# Optimizing a Trainium2 kernel written in Bass

```python
import jax, jax.numpy as jnp
from jax import lax
import numpy as np
import math

D_MODEL = 1024
BATCH = 1
SEQ = 256
DEPTH = 2

POOL_WINDOWS = (2, 4, 8, 16)
POOL_WIDTH = 512
POOL_GROUP = POOL_WIDTH // len(POOL_WINDOWS)
N_HEADS = 8
HEAD_DIM = 64
ATTN_WIDTH = N_HEADS * HEAD_DIM
MOBA_BLOCK = 256
MOBA_TOP_K = 3
Q_CHUNK = 64
ROPE_THETA = 10000.0
N_BRANCH = 2
IN_WIDTH = POOL_WIDTH + 3 * ATTN_WIDTH + N_BRANCH * D_MODEL
D_FF = 2816
EPS = 1e-6
NEG = -1e30


def rms_norm(x, g):
    xf = x.astype(jnp.float32)
    y = xf * lax.rsqrt(jnp.mean(xf * xf, axis=-1, keepdims=True) + EPS)
    return (y * g.astype(jnp.float32)).astype(x.dtype)

def swiglu(h, w_gate_up, w_down):
    a, b = jnp.split(h @ w_gate_up, 2, axis=-1)
    return (jax.nn.silu(a) * b) @ w_down

def rope(x):
    S, Dh = x.shape[1], x.shape[-1]
    half = Dh // 2
    inv_freq = 1.0 / (ROPE_THETA ** (jnp.arange(half, dtype=jnp.float32) * (2.0 / Dh)))
    ang = jnp.arange(S, dtype=jnp.float32)[:, None] * inv_freq[None, :]
    cos = jnp.cos(ang)[None, :, None, :]
    sin = jnp.sin(ang)[None, :, None, :]
    xf = x.astype(jnp.float32)
    x1, x2 = xf[..., :half], xf[..., half:]
    out = jnp.concatenate([x1 * cos - x2 * sin, x2 * cos + x1 * sin], axis=-1)
    return out.astype(x.dtype)

def multiscale_pool(u, w_grp, scale):
    B, S, _ = u.shape
    G = len(POOL_WINDOWS)
    uf = u.astype(jnp.float32).reshape(B, S, G, POOL_GROUP)
    csum = jnp.concatenate([jnp.zeros((B, 1, G, POOL_GROUP), jnp.float32),
                            jnp.cumsum(uf, axis=1)], axis=1)
    t = jnp.arange(S)
    means = []
    for g, w in enumerate(POOL_WINDOWS):
        lo = jnp.maximum(t + 1 - w, 0)
        cnt = (t + 1 - lo).astype(jnp.float32)
        means.append((csum[:, 1:, g] - csum[:, lo, g]) / cnt[None, :, None])
    pooled = jnp.stack(means, axis=2)
    d = (pooled - uf).astype(u.dtype)
    y = jnp.einsum('bsgc,gcd->bsgd', d, w_grp).reshape(B, S, POOL_WIDTH)
    return y * scale

def moba_attention(q, k, v):
    B, S, H, Dh = q.shape
    nb = -(-S // MOBA_BLOCK)
    pad = nb * MOBA_BLOCK - S
    kp = jnp.pad(k, ((0, 0), (0, pad), (0, 0), (0, 0)))
    vp = jnp.pad(v, ((0, 0), (0, pad), (0, 0), (0, 0)))
    kb = kp.reshape(B, nb, MOBA_BLOCK, H, Dh).transpose(0, 3, 1, 2, 4)
    vb = vp.reshape(B, nb, MOBA_BLOCK, H, Dh).transpose(0, 3, 1, 2, 4)
    kbar = jnp.mean(kb.astype(jnp.float32), axis=3)
    nc = S // Q_CHUNK
    qc = q.reshape(B, nc, Q_CHUNK, H, Dh).transpose(1, 0, 3, 2, 4)
    k_eff = min(MOBA_TOP_K, nb)
    scale = Dh ** -0.5
    bi = jnp.arange(B)[:, None, None, None]
    hi = jnp.arange(H)[None, :, None, None]
    blk_ids = jnp.arange(nb)

    def one_chunk(args):
        qi, ci = args
        q0 = ci * Q_CHUNK
        qblk = q0 // MOBA_BLOCK
        qpos = q0 + jnp.arange(Q_CHUNK)
        gate = jnp.einsum('bhqd,bhnd->bhqn', qi.astype(jnp.float32), kbar)
        gate = jnp.where(blk_ids < qblk, gate, NEG)
        _, sel = lax.top_k(gate, k_eff)
        valid = sel < qblk
        ksel = kb[bi, hi, sel]
        vsel = vb[bi, hi, sel]
        kown = lax.dynamic_index_in_dim(kb, qblk, axis=2, keepdims=False)
        vown = lax.dynamic_index_in_dim(vb, qblk, axis=2, keepdims=False)
        s_sel = jnp.einsum('bhqd,bhqknd->bhqkn', qi, ksel).astype(jnp.float32) * scale
        s_sel = jnp.where(valid[..., None], s_sel, NEG).reshape(B, H, Q_CHUNK, k_eff * MOBA_BLOCK)
        kpos = qblk * MOBA_BLOCK + jnp.arange(MOBA_BLOCK)
        s_own = jnp.einsum('bhqd,bhnd->bhqn', qi, kown).astype(jnp.float32) * scale
        s_own = jnp.where(kpos[None, :] <= qpos[:, None], s_own, NEG)
        p = jax.nn.softmax(jnp.concatenate([s_sel, s_own], axis=-1), axis=-1).astype(v.dtype)
        p_sel = p[..., :k_eff * MOBA_BLOCK].reshape(B, H, Q_CHUNK, k_eff, MOBA_BLOCK)
        p_own = p[..., k_eff * MOBA_BLOCK:]
        return (jnp.einsum('bhqkn,bhqknd->bhqd', p_sel, vsel)
                + jnp.einsum('bhqn,bhnd->bhqd', p_own, vown))

    out = lax.map(one_chunk, (qc, jnp.arange(nc)))
    return out.transpose(1, 0, 3, 2, 4).reshape(B, S, H * Dh)

def hybrid_layer(x, ffn1_norm, ffn1_w_gate_up, ffn1_w_down, mix_norm, w_in, b_gate,
                 pool_w, pool_scale, q_norm, k_norm, w_branch_pool, w_branch_attn, w_out,
                 ffn2_norm, ffn2_w_gate_up, ffn2_w_down):
    B, S, D = x.shape
    x = x + 0.5 * swiglu(rms_norm(x, ffn1_norm), ffn1_w_gate_up, ffn1_w_down)
    h = rms_norm(x, mix_norm)
    z = h @ w_in
    o1 = POOL_WIDTH
    o2 = o1 + ATTN_WIDTH
    o3 = o2 + ATTN_WIDTH
    o4 = o3 + ATTN_WIDTH
    u, q, k, v, gl = z[..., :o1], z[..., o1:o2], z[..., o2:o3], z[..., o3:o4], z[..., o4:]
    y_pool = multiscale_pool(u, pool_w, pool_scale)
    q = rope(rms_norm(q.reshape(B, S, N_HEADS, HEAD_DIM), q_norm))
    k = rope(rms_norm(k.reshape(B, S, N_HEADS, HEAD_DIM), k_norm))
    v = v.reshape(B, S, N_HEADS, HEAD_DIM)
    y_attn = moba_attention(q, k, v)
    gates = jax.nn.sigmoid(gl + b_gate).reshape(B, S, N_BRANCH, D)
    merged = gates[:, :, 0] * (y_pool @ w_branch_pool) + gates[:, :, 1] * (y_attn @ w_branch_attn)
    x = x + merged @ w_out
    x = x + 0.5 * swiglu(rms_norm(x, ffn2_norm), ffn2_w_gate_up, ffn2_w_down)
    return x

def first_inputs(seed: int = 0) -> dict:
    key = jax.random.key(seed)
    ks = jax.random.split(key, 18)
    f32 = jnp.float32

    def w(k, shape, fan_in):
        return jax.random.normal(k, shape, f32) * (fan_in ** -0.5)

    def gain(k, shape):
        return 1.0 + 0.1 * jax.random.normal(k, shape, f32)

    L = DEPTH
    return {
        "x": jax.random.normal(ks[0], (BATCH, SEQ, D_MODEL), f32),
        "ffn1_norm": gain(ks[1], (L, D_MODEL)),
        "ffn1_w_gate_up": w(ks[2], (L, D_MODEL, 2 * D_FF), D_MODEL),
        "ffn1_w_down": w(ks[3], (L, D_FF, D_MODEL), D_FF),
        "mix_norm": gain(ks[4], (L, D_MODEL)),
        "w_in": w(ks[5], (L, D_MODEL, IN_WIDTH), D_MODEL),
        "b_gate": 0.1 * jax.random.normal(ks[6], (L, N_BRANCH * D_MODEL), f32),
        "pool_w": w(ks[7], (L, len(POOL_WINDOWS), POOL_GROUP, POOL_GROUP), POOL_GROUP),
        "pool_scale": gain(ks[8], (L, POOL_WIDTH)),
        "q_norm": gain(ks[9], (L, HEAD_DIM)),
        "k_norm": gain(ks[10], (L, HEAD_DIM)),
        "w_branch_pool": w(ks[11], (L, POOL_WIDTH, D_MODEL), POOL_WIDTH),
        "w_branch_attn": w(ks[12], (L, ATTN_WIDTH, D_MODEL), ATTN_WIDTH),
        "w_out": w(ks[13], (L, D_MODEL, D_MODEL), D_MODEL),
        "ffn2_norm": gain(ks[14], (L, D_MODEL)),
        "ffn2_w_gate_up": w(ks[15], (L, D_MODEL, 2 * D_FF), D_MODEL),
        "ffn2_w_down": w(ks[16], (L, D_FF, D_MODEL), D_FF),
    }

def first_block(x, ffn1_norm, ffn1_w_gate_up, ffn1_w_down, mix_norm, w_in, b_gate,
              pool_w, pool_scale, q_norm, k_norm, w_branch_pool, w_branch_attn, w_out,
              ffn2_norm, ffn2_w_gate_up, ffn2_w_down):
    for l in range(DEPTH):
        x = hybrid_layer(x, ffn1_norm[l], ffn1_w_gate_up[l], ffn1_w_down[l], mix_norm[l],
                         w_in[l], b_gate[l], pool_w[l], pool_scale[l], q_norm[l], k_norm[l],
                         w_branch_pool[l], w_branch_attn[l], w_out[l],
                         ffn2_norm[l], ffn2_w_gate_up[l], ffn2_w_down[l])
    return x


DEPTH_2 = 1

NEG_2 = -1e30
M_HEADS = 4
M_DQK = 64
M_DV = 128
M_CHUNK = 64
M_CONV = 4
M_QK = M_HEADS * M_DQK
M_V = M_HEADS * M_DV
N_KV = 2
N_HG = N_HEADS // N_KV
N_DH = 64
N_Q = N_HEADS * N_DH
N_KVW = N_KV * N_DH
CMP_LEN = 32
CMP_STRIDE = 16
CMP_HIDDEN = 256
SEL_BLOCK = 64
SEL_TOPN = 16
WINDOW = 512
Q_BLOCK = 128
FORCE_BONUS = 1e4
FFN_CONV = 3
IN_SIZES = (M_QK, M_QK, M_V, M_V, M_HEADS, M_HEADS,
            N_Q, N_KVW, N_KVW, N_KVW, N_KVW, N_KVW, N_KVW, 3 * N_HEADS,
            D_MODEL, D_MODEL)
D_IN = sum(IN_SIZES)


def rmsnorm(x, w):
    xf = x.astype(jnp.float32)
    y = xf * lax.rsqrt(jnp.mean(xf * xf, axis=-1, keepdims=True) + EPS)
    return (y * w.astype(jnp.float32)).astype(x.dtype)

def causal_dwconv(x, w, b):
    K = w.shape[0]
    S = x.shape[1]
    xp = jnp.pad(x, ((0, 0), (K - 1, 0), (0, 0)))
    y = xp[:, 0:S] * w[0]
    for k in range(1, K):
        y = y + xp[:, k:k + S] * w[k]
    return y + b

def rope_tables(S):
    pos = jnp.arange(S, dtype=jnp.float32)
    inv = ROPE_THETA ** (-jnp.arange(0, N_DH, 2, dtype=jnp.float32) / N_DH)
    ang = pos[:, None] * inv[None, :]
    return jnp.cos(ang), jnp.sin(ang)

def apply_rope(x, cos, sin):
    x1, x2 = jnp.split(x.astype(jnp.float32), 2, axis=-1)
    c = cos[None, :, None, :]
    s = sin[None, :, None, :]
    return jnp.concatenate([x1 * c - x2 * s, x2 * c + x1 * s], axis=-1).astype(x.dtype)

def mlstm_chunkwise(q, k, v, i_pre, logf):
    B, NH, S, DQK = q.shape
    DV = v.shape[-1]
    L = M_CHUNK
    NC = S // L
    q = q.reshape(B, NH, NC, L, DQK) * (DQK ** -0.5)
    k = k.reshape(B, NH, NC, L, DQK)
    v = v.reshape(B, NH, NC, L, DV)
    i_pre = i_pre.reshape(B, NH, NC, L)
    logf = logf.reshape(B, NH, NC, L)
    b = jnp.cumsum(logf, axis=-1)
    g = b[..., -1]
    a = g[..., None] - b + i_pre
    a_max = jnp.max(a, axis=-1)
    w = jnp.exp(a - a_max[..., None])
    dC = jnp.einsum('bhcl,bhcld,bhcle->bhcde', w, k, v)
    dn = jnp.einsum('bhcl,bhcld->bhcd', w, k)

    def step(carry, inp):
        C, n, m = carry
        dC_c, dn_c, g_c, am_c = inp
        m_new = jnp.maximum(g_c + m, am_c)
        decay = jnp.exp(g_c + m - m_new)
        scl = jnp.exp(am_c - m_new)
        C_new = decay[..., None, None] * C + scl[..., None, None] * dC_c
        n_new = decay[..., None] * n + scl[..., None] * dn_c
        return (C_new, n_new, m_new), (C, n, m)

    init = (jnp.zeros((B, NH, DQK, DV), jnp.float32),
            jnp.zeros((B, NH, DQK), jnp.float32),
            jnp.zeros((B, NH), jnp.float32))
    xs = (jnp.moveaxis(dC, 2, 0), jnp.moveaxis(dn, 2, 0),
          jnp.moveaxis(g, 2, 0), jnp.moveaxis(a_max, 2, 0))
    _, (C_prev, n_prev, m_prev) = lax.scan(step, init, xs)
    C_prev = jnp.moveaxis(C_prev, 0, 2)
    n_prev = jnp.moveaxis(n_prev, 0, 2)
    m_prev = jnp.moveaxis(m_prev, 0, 2)

    causal = jnp.tril(jnp.ones((L, L), dtype=bool))
    D = b[..., :, None] - b[..., None, :] + i_pre[..., None, :]
    D = jnp.where(causal, D, NEG_2)
    inter = b + m_prev[..., None]
    m_t = jnp.maximum(inter, jnp.max(D, axis=-1))
    Dw = jnp.exp(D - m_t[..., None])
    s = jnp.einsum('bhctd,bhcsd->bhcts', q, k) * Dw
    isc = jnp.exp(inter - m_t)
    num = isc[..., None] * jnp.einsum('bhctd,bhcde->bhcte', q, C_prev) \
        + jnp.einsum('bhcts,bhcse->bhcte', s, v)
    den = isc * jnp.einsum('bhctd,bhcd->bhct', q, n_prev) + jnp.sum(s, axis=-1)
    h = num / jnp.maximum(jnp.abs(den), jnp.exp(-m_t))[..., None]
    return h.reshape(B, NH, S, DV)

def compress_blocks(kv, pe, w1, w2):
    B, G, S, dh = kv.shape
    ncmp = (S - CMP_LEN) // CMP_STRIDE + 1
    idx = (jnp.arange(ncmp) * CMP_STRIDE)[:, None] + jnp.arange(CMP_LEN)[None, :]
    blk = kv[:, :, idx] + pe
    flat = blk.reshape(B, G, ncmp, CMP_LEN * dh)
    return jax.nn.gelu(flat @ w1, approximate=False) @ w2

def masked_softmax(s, mask):
    s = jnp.where(mask, s.astype(jnp.float32), NEG_2)
    p = jax.nn.softmax(s, axis=-1)
    return jnp.where(mask, p, 0.0)

def nsa_branches(q, kc, vc, ks, vs, kw, vw):
    B, G, HG, S, dh = q.shape
    nqb = S // Q_BLOCK
    nsel = S // SEL_BLOCK
    topn = min(SEL_TOPN, nsel)
    ncmp = kc.shape[2]
    scale = dh ** -0.5
    cstart = jnp.arange(ncmp) * CMP_STRIDE
    cend = cstart + CMP_LEN - 1
    sstart = jnp.arange(nsel) * SEL_BLOCK
    send = sstart + SEL_BLOCK - 1
    overlap = ((cstart[:, None] <= send[None, :]) & (cend[:, None] >= sstart[None, :])).astype(jnp.float32)
    ksb = ks.reshape(B, G, nsel, SEL_BLOCK, dh)
    vsb = vs.reshape(B, G, nsel, SEL_BLOCK, dh)
    kwp = jnp.pad(kw, ((0, 0), (0, 0), (WINDOW, 0), (0, 0)))
    vwp = jnp.pad(vw, ((0, 0), (0, 0), (WINDOW, 0), (0, 0)))
    qblocks = jnp.moveaxis(q.reshape(B, G, HG, nqb, Q_BLOCK, dh), 3, 0)
    gather = jax.vmap(jax.vmap(lambda blocks, ix: blocks[ix]))
    jsel = jnp.arange(nsel)
    win_off = jnp.arange(Q_BLOCK + WINDOW)
    sb_off = jnp.arange(SEL_BLOCK)

    def one_block(args):
        qi, qb = args
        s0 = qi * Q_BLOCK
        tpos = s0 + jnp.arange(Q_BLOCK)
        cmask = cend[None, :] <= tpos[:, None]
        pc = masked_softmax(jnp.einsum('bghqd,bgnd->bghqn', qb, kc) * scale, cmask)
        o_cmp = jnp.einsum('bghqn,bgnd->bghqd', pc.astype(vc.dtype), vc)
        imp = jnp.einsum('bghqn,nj->bgqj', pc, overlap)
        cur = tpos // SEL_BLOCK
        forced = (jsel[None, :] == 0) | (jsel[None, :] == cur[:, None]) | (jsel[None, :] == cur[:, None] - 1)
        imp = jnp.where(forced, FORCE_BONUS, imp)
        imp = jnp.where(jsel[None, :] > cur[:, None], NEG_2, imp)
        _, idx = lax.top_k(imp, topn)
        ksel = gather(ksb, idx).reshape(B, G, Q_BLOCK, topn * SEL_BLOCK, dh)
        vsel = gather(vsb, idx).reshape(B, G, Q_BLOCK, topn * SEL_BLOCK, dh)
        spos = (idx[..., None] * SEL_BLOCK + sb_off).reshape(B, G, Q_BLOCK, topn * SEL_BLOCK)
        smask = (spos <= tpos[None, None, :, None])[:, :, None]
        ps = masked_softmax(jnp.einsum('bghqd,bgqmd->bghqm', qb, ksel) * scale, smask)
        o_slc = jnp.einsum('bghqm,bgqmd->bghqd', ps.astype(vsel.dtype), vsel)
        kwin = lax.dynamic_slice_in_dim(kwp, s0, Q_BLOCK + WINDOW, axis=2)
        vwin = lax.dynamic_slice_in_dim(vwp, s0, Q_BLOCK + WINDOW, axis=2)
        kpos = s0 - WINDOW + win_off
        wmask = (kpos[None, :] <= tpos[:, None]) & (kpos[None, :] > tpos[:, None] - WINDOW) & (kpos[None, :] >= 0)
        pw = masked_softmax(jnp.einsum('bghqd,bgkd->bghqk', qb, kwin) * scale, wmask)
        o_win = jnp.einsum('bghqk,bgkd->bghqd', pw.astype(vwin.dtype), vwin)
        return o_cmp, o_slc, o_win

    o_cmp, o_slc, o_win = lax.map(one_block, (jnp.arange(nqb), qblocks))
    unblock = lambda o: jnp.moveaxis(o, 0, 3).reshape(B, G, HG, S, dh)
    return unblock(o_cmp), unblock(o_slc), unblock(o_win)

def hybrid_layer_2(x, cos, sin, norm1_w, w_in, m_conv_w, m_conv_b, m_igate_b, m_fgate_b, m_out_norm_w,
                 q_norm_w, kcmp_norm_w, kslc_norm_w, kwin_norm_w,
                 cmp_k_pe, cmp_k_w1, cmp_k_w2, cmp_v_pe, cmp_v_w1, cmp_v_w2,
                 w_up_m, w_up_n, merge_gate_b, w_out,
                 norm2_w, ffn_w_up, ffn_conv_w, ffn_conv_b, ffn_w_down):
    B, S, _ = x.shape
    h = rmsnorm(x, norm1_w)
    proj = h @ w_in
    split_pts = np.cumsum(IN_SIZES)[:-1].tolist()
    (mq, mk, mv, mo, mi, mf, nq, kc, vc, ks, vs, kw, vw, ng, gm, gn) = jnp.split(proj, split_pts, axis=-1)

    qk = jax.nn.silu(causal_dwconv(jnp.concatenate([mq, mk], axis=-1), m_conv_w, m_conv_b))
    mq, mk = jnp.split(qk, 2, axis=-1)
    to_mheads = lambda t, d: t.reshape(B, S, M_HEADS, d).transpose(0, 2, 1, 3).astype(jnp.float32)
    i_pre = (mi + m_igate_b).astype(jnp.float32).transpose(0, 2, 1)
    logf = jax.nn.log_sigmoid((mf + m_fgate_b).astype(jnp.float32)).transpose(0, 2, 1)
    hm = mlstm_chunkwise(to_mheads(mq, M_DQK), to_mheads(mk, M_DQK), to_mheads(mv, M_DV), i_pre, logf)
    hm = rmsnorm(hm.transpose(0, 2, 1, 3), m_out_norm_w)
    hm = hm.reshape(B, S, M_V).astype(x.dtype) * jax.nn.sigmoid(mo)

    qn = apply_rope(rmsnorm(nq.reshape(B, S, N_HEADS, N_DH), q_norm_w), cos, sin)
    kv_heads = lambda t: t.reshape(B, S, N_KV, N_DH)
    to_groups = lambda t: t.transpose(0, 2, 1, 3)
    kc_t = to_groups(apply_rope(rmsnorm(kv_heads(kc), kcmp_norm_w), cos, sin))
    ks_t = to_groups(apply_rope(rmsnorm(kv_heads(ks), kslc_norm_w), cos, sin))
    kw_t = to_groups(apply_rope(rmsnorm(kv_heads(kw), kwin_norm_w), cos, sin))
    vc_t = to_groups(kv_heads(vc))
    vs_t = to_groups(kv_heads(vs))
    vw_t = to_groups(kv_heads(vw))
    qg = qn.reshape(B, S, N_KV, N_HG, N_DH).transpose(0, 2, 3, 1, 4)
    kcmp = compress_blocks(kc_t, cmp_k_pe, cmp_k_w1, cmp_k_w2)
    vcmp = compress_blocks(vc_t, cmp_v_pe, cmp_v_w1, cmp_v_w2)
    o_cmp, o_slc, o_win = nsa_branches(qg, kcmp, vcmp, ks_t, vs_t, kw_t, vw_t)
    gates = jax.nn.sigmoid(ng.reshape(B, S, N_KV, N_HG, 3).transpose(0, 2, 3, 1, 4))
    on = gates[..., 0:1] * o_cmp + gates[..., 1:2] * o_slc + gates[..., 2:3] * o_win
    on = on.transpose(0, 3, 1, 2, 4).reshape(B, S, N_Q)

    y = jax.nn.sigmoid(gm + merge_gate_b[0]) * (hm @ w_up_m) \
        + jax.nn.sigmoid(gn + merge_gate_b[1]) * (on @ w_up_n)
    x = x + y @ w_out

    h2 = rmsnorm(x, norm2_w)
    a, v = jnp.split(h2 @ ffn_w_up, 2, axis=-1)
    a = jax.nn.gelu(causal_dwconv(a, ffn_conv_w, ffn_conv_b), approximate=False)
    return x + (a * v) @ ffn_w_down

def second_inputs(seed: int = 0) -> dict:
    key = jax.random.key(seed)
    ks = jax.random.split(key, 32)
    f32 = jnp.float32
    nrm = lambda k, shape, s: jax.random.normal(k, shape, f32) * s
    gain = lambda k, shape: 1.0 + 0.02 * jax.random.normal(k, shape, f32)
    Ld = DEPTH_2
    return {
        "x": nrm(ks[0], (BATCH, SEQ, D_MODEL), 1.0),
        "norm1_w": gain(ks[1], (Ld, D_MODEL)),
        "w_in": nrm(ks[2], (Ld, D_MODEL, D_IN), D_MODEL ** -0.5),
        "m_conv_w": nrm(ks[3], (Ld, M_CONV, 2 * M_QK), M_CONV ** -0.5),
        "m_conv_b": nrm(ks[4], (Ld, 2 * M_QK), 0.01),
        "m_igate_b": nrm(ks[5], (Ld, M_HEADS), 0.1),
        "m_fgate_b": jnp.linspace(3.0, 6.0, M_HEADS, dtype=f32)[None, :] + nrm(ks[6], (Ld, M_HEADS), 0.01),
        "m_out_norm_w": gain(ks[7], (Ld, M_HEADS, M_DV)),
        "q_norm_w": gain(ks[8], (Ld, N_DH)),
        "kcmp_norm_w": gain(ks[9], (Ld, N_DH)),
        "kslc_norm_w": gain(ks[10], (Ld, N_DH)),
        "kwin_norm_w": gain(ks[11], (Ld, N_DH)),
        "cmp_k_pe": nrm(ks[12], (Ld, CMP_LEN, N_DH), 0.02),
        "cmp_k_w1": nrm(ks[13], (Ld, CMP_LEN * N_DH, CMP_HIDDEN), (CMP_LEN * N_DH) ** -0.5),
        "cmp_k_w2": nrm(ks[14], (Ld, CMP_HIDDEN, N_DH), CMP_HIDDEN ** -0.5),
        "cmp_v_pe": nrm(ks[15], (Ld, CMP_LEN, N_DH), 0.02),
        "cmp_v_w1": nrm(ks[16], (Ld, CMP_LEN * N_DH, CMP_HIDDEN), (CMP_LEN * N_DH) ** -0.5),
        "cmp_v_w2": nrm(ks[17], (Ld, CMP_HIDDEN, N_DH), CMP_HIDDEN ** -0.5),
        "w_up_m": nrm(ks[18], (Ld, M_V, D_MODEL), M_V ** -0.5),
        "w_up_n": nrm(ks[19], (Ld, N_Q, D_MODEL), N_Q ** -0.5),
        "merge_gate_b": nrm(ks[20], (Ld, 2, D_MODEL), 0.01),
        "w_out": nrm(ks[21], (Ld, D_MODEL, D_MODEL), D_MODEL ** -0.5),
        "norm2_w": gain(ks[22], (Ld, D_MODEL)),
        "ffn_w_up": nrm(ks[23], (Ld, D_MODEL, 2 * D_FF), D_MODEL ** -0.5),
        "ffn_conv_w": nrm(ks[24], (Ld, FFN_CONV, D_FF), FFN_CONV ** -0.5),
        "ffn_conv_b": nrm(ks[25], (Ld, D_FF), 0.01),
        "ffn_w_down": nrm(ks[26], (Ld, D_FF, D_MODEL), D_FF ** -0.5),
    }

def second_block(x, norm1_w, w_in, m_conv_w, m_conv_b, m_igate_b, m_fgate_b, m_out_norm_w,
              q_norm_w, kcmp_norm_w, kslc_norm_w, kwin_norm_w,
              cmp_k_pe, cmp_k_w1, cmp_k_w2, cmp_v_pe, cmp_v_w1, cmp_v_w2,
              w_up_m, w_up_n, merge_gate_b, w_out,
              norm2_w, ffn_w_up, ffn_conv_w, ffn_conv_b, ffn_w_down):
    cos, sin = rope_tables(x.shape[1])
    layer_params = (norm1_w, w_in, m_conv_w, m_conv_b, m_igate_b, m_fgate_b, m_out_norm_w,
                    q_norm_w, kcmp_norm_w, kslc_norm_w, kwin_norm_w,
                    cmp_k_pe, cmp_k_w1, cmp_k_w2, cmp_v_pe, cmp_v_w1, cmp_v_w2,
                    w_up_m, w_up_n, merge_gate_b, w_out,
                    norm2_w, ffn_w_up, ffn_conv_w, ffn_conv_b, ffn_w_down)
    for layer in range(DEPTH_2):
        x = hybrid_layer_2(x, cos, sin, *[p[layer] for p in layer_params])
    return x


def setup_inputs(seed=0):
    out = dict(first_inputs(seed))
    for name, value in second_inputs(seed + 1).items():
        if name != "x":
            out[name + "_2"] = value
    return out


def reference(
    x, ffn1_norm, ffn1_w_gate_up, ffn1_w_down, mix_norm, w_in, b_gate, pool_w, pool_scale,
    q_norm, k_norm, w_branch_pool, w_branch_attn, w_out, ffn2_norm, ffn2_w_gate_up, ffn2_w_down,
    norm1_w_2, w_in_2, m_conv_w_2, m_conv_b_2, m_igate_b_2, m_fgate_b_2, m_out_norm_w_2,
    q_norm_w_2, kcmp_norm_w_2, kslc_norm_w_2, kwin_norm_w_2, cmp_k_pe_2, cmp_k_w1_2, cmp_k_w2_2,
    cmp_v_pe_2, cmp_v_w1_2, cmp_v_w2_2, w_up_m_2, w_up_n_2, merge_gate_b_2, w_out_2, norm2_w_2,
    ffn_w_up_2, ffn_conv_w_2, ffn_conv_b_2, ffn_w_down_2,
):
    x = first_block(
        x, ffn1_norm, ffn1_w_gate_up, ffn1_w_down, mix_norm, w_in, b_gate, pool_w, pool_scale,
        q_norm, k_norm, w_branch_pool, w_branch_attn, w_out, ffn2_norm, ffn2_w_gate_up,
        ffn2_w_down,
    )
    return second_block(
        x, norm1_w_2, w_in_2, m_conv_w_2, m_conv_b_2, m_igate_b_2, m_fgate_b_2, m_out_norm_w_2,
        q_norm_w_2, kcmp_norm_w_2, kslc_norm_w_2, kwin_norm_w_2, cmp_k_pe_2, cmp_k_w1_2,
        cmp_k_w2_2, cmp_v_pe_2, cmp_v_w1_2, cmp_v_w2_2, w_up_m_2, w_up_n_2, merge_gate_b_2,
        w_out_2, norm2_w_2, ffn_w_up_2, ffn_conv_w_2, ffn_conv_b_2, ffn_w_down_2,
    )


_drawn_inputs = setup_inputs


def setup_inputs(seed=0):
    import zlib

    import numpy as np

    out = dict(_drawn_inputs(seed))
    spreads = {}
    factors = {'q_norm': 3.735,
     'k_norm': 3.599,
     'norm1_w_2': 6.146,
     'm_conv_b_2': 8.0,
     'm_igate_b_2': 64.0,
     'm_out_norm_w_2': 27.969,
     'q_norm_w_2': 8.0,
     'kcmp_norm_w_2': 8.0,
     'kslc_norm_w_2': 8.0,
     'kwin_norm_w_2': 8.0,
     'cmp_k_pe_2': 8.0,
     'cmp_v_pe_2': 39.444,
     'merge_gate_b_2': 26.76,
     'norm2_w_2': 4.826,
     'ffn_conv_b_2': 27.904}
    for name, (base, spread) in spreads.items():
        noise = np.random.default_rng([zlib.crc32(name.encode()), seed]).standard_normal(out[name].shape)
        drawn = base * np.exp(spread * noise) if base else spread * noise
        out[name] = __import__('jax').numpy.asarray(drawn.astype(out[name].dtype))
    for name, factor in factors.items():
        out[name] = (out[name] * factor).astype(out[name].dtype)
    return out
```

```python
import math
from contextlib import ExitStack

import numpy as np

import concourse.bass as bass
from concourse import mybir

ALU = mybir.AluOpType
ACT = mybir.ActivationFunctionType
F32 = mybir.dt.float32
F32R = mybir.dt.float32r
AX = mybir.AxisListType.X

P = 128
S = 256
D = 1024
KD = D // P
DFF = 2816
NF = DFF // P
EPS = 1e-6
TW = 1024
NRAW = 5
NSPL = 6
AHEAD = 4
NEG = -1.0e30


def constants():
    c = {}
    c["ident"] = np.eye(P, dtype=np.float32)
    t = np.arange(P)
    tri = np.where(t[None, :] > t[:, None], np.float32(NEG), np.float32(0)).astype(np.float32)
    c["cmask"] = np.concatenate([tri, np.zeros((P, P), np.float32), tri], 1)
    c["bigT"] = np.where(t[:, None] > t[None, :], np.float32(1e30), np.float32(0)).astype(np.float32)
    half = 32
    inv = (np.float32(1.0) / (np.float32(10000.0) ** (np.arange(half, dtype=np.float32) * np.float32(2.0 / 64)))).astype(np.float32)
    ang = (np.arange(S, dtype=np.float32)[:, None] * inv[None, :]).astype(np.float32)
    cos, sin = np.cos(ang).astype(np.float32), np.sin(ang).astype(np.float32)
    cs = np.concatenate([cos, cos], 1).reshape(2, P, 64)
    sn = np.concatenate([-sin, sin], 1).reshape(2, P, 64)
    c["cos"] = cs.transpose(1, 0, 2).reshape(P, 128)
    c["sin"] = sn.transpose(1, 0, 2).reshape(P, 128)
    pm = []
    tt = np.arange(S)
    for w in (2, 4, 8, 16):
        lo = np.maximum(tt + 1 - w, 0)
        cnt = (tt + 1 - lo).astype(np.float32)
        s = np.arange(S)[:, None]
        m = np.where((s >= lo[None, :]) & (s <= tt[None, :]), np.float32(1) / cnt[None, :], np.float32(0))
        m = m - np.eye(S)
        pm += [m[0:P, :], m[P:S, P:S]]
    c["pool"] = np.concatenate(pm, 1).astype(np.float32)
    n = np.arange(15)
    cm = np.zeros((P, 2, 16), np.float32)
    for k in range(2):
        cm[:, k, :15] = (16 * n[None, :] + 31 <= (k * P + t)[:, None])
    c["cm01"] = cm.reshape(P, 32)
    c["cmneg"] = ((cm.astype(np.float64) - 1) * 1e30).astype(np.float32).reshape(P, 32)
    r = np.zeros((P, 2, 8, 16), np.float32)
    for h in range(8):
        for i in range(15):
            r[i, h // 4, h, i] = 1
    c["rep"] = r.reshape(P, 256)
    bd = np.zeros((8, 16, 4, 2, 64), np.float32)
    for h in range(8):
        bd[h, :, h // 2, h % 2, :] = 1
    c["bd"] = bd.reshape(P, 512)
    sel = np.zeros((P, 4, P), np.float32)
    for h in range(4):
        sel[h, h, :] = 1
    c["sel"] = sel.reshape(P, 512)
    names, at, off = [k for k in c if k != "pool"] + ["pool"], {}, 0
    for k in names:
        at[k] = (off, off + c[k].shape[1])
        off += c[k].shape[1]
    return np.ascontiguousarray(np.concatenate([c[k] for k in names], 1)), at


def params_layout():
    at, off = {}, 0
    for name, n in ([(f"bg{l}", 16) for l in range(2)] + [(f"ps{l}", 4) for l in range(2)]
                    + [(f"qn{l}", 64) for l in range(2)] + [(f"kn{l}", 64) for l in range(2)]
                    + [("mg", 16), ("cw", 16), ("cb", 4), ("ib", 1), ("fb", 1), ("on", 512), ("qn2", 64),
                       ("kn3", 192), ("kpe", 16), ("vpe", 16), ("fw", 3 * NF), ("fbias", NF),
                       ("kw2", 256), ("vw2", 256)]):
        at[name] = (off, off + n)
        off += n
    return at, off



def a_group(n):
    per = TW // n
    return [(k, min(per, KD - k)) for k in range(0, KD, per)]


L2_GROUPS = [("k3", 512), ("v3", 288), ("nq", 512), ("mv", 512), ("mo", 512)]


def tile_plan():
    plan = []

    def ffn(tag):
        for i in range(NF + 2):
            if i < NF:
                plan.extend([(f"{tag}a{i}", TW, True), (f"{tag}b{i}", TW, True)])
            if i >= 2:
                plan.append((f"{tag}d{i - 2}", TW, True))

    def tail(tag):
        for i in range(KD + 1):
            if i < KD:
                plan.append((f"{tag}br{i}", TW, True))
            if i >= 1:
                plan.append((f"{tag}wo{i - 1}", TW, True))

    for l in range(2):
        ffn(f"L{l}f1")
        for g in ("k", "q", "v", "u"):
            for k, m in a_group(512):
                plan.append((f"L{l}{g}{k}", m * 512, True))
        for f in range(KD):
            plan.extend([(f"L{l}g0{f}", TW, True), (f"L{l}g1{f}", TW, True)])
        tail(f"L{l}")
        ffn(f"L{l}f2")
    for g, n in L2_GROUPS[:3]:
        for k, m in a_group(n):
            plan.append((f"M{g}{k}", m * n, True))
    for f in range(4):
        plan.append((f"Mqk{f}", TW, True))
    w1 = 0
    for g, n in L2_GROUPS[3:]:
        for k, m in a_group(n):
            plan.append((f"M{g}{k}", m * n, True))
            plan.append((f"M{'kv'[w1 // 4]}w1{w1 % 4}", TW, False))
            w1 += 1
    for f in range(2 * KD):
        plan.append((f"Mg{f % 2}{f // 2}", TW, True))
    tail("M")
    ffn("Mf")
    off, out = 0, []
    for name, n, split in plan:
        out.append((name, n, split, off))
        off += n
    return out, off


class Op:

    def __init__(self, eng, emit, waits, sem=None, value=0):
        self.eng, self.emit, self.waits, self.sem, self.value = eng, emit, waits, sem, value
        self.signals = sem is not None


class Queues:

    def __init__(self):
        self.q = {e: [] for e in ("pe", "act", "dve", "pool", "sp")}
        self.dma_count = {}

    def put(self, eng, emit, *waits):
        flat, todo = [], list(waits)
        while todo:
            w = todo.pop()
            if isinstance(w, (list, tuple)):
                todo.extend(w)
            else:
                w.signals = True
                flat.append(w)
        op = Op(eng, emit, flat)
        self.q[eng].append(op)
        return op

    def dma(self, sem, emit, *waits, eng="sp"):
        op = self.put(eng, emit, *waits)
        self.dma_count[sem] = self.dma_count.get(sem, 0) + 16
        op.sem, op.value, op.signals = sem, self.dma_count[sem], True
        return op

    def number(self):
        for eng, ops in self.q.items():
            n = 0
            for op in ops:
                if op.signals and op.sem is None:
                    n += 1
                    op.sem, op.value = eng, n

    def run(self, eng, handle, sems):
        seen = {}
        for op in self.q[eng]:
            need = {}
            for w in op.waits:
                need[w.sem] = max(need.get(w.sem, 0), w.value)
            for s, v in need.items():
                if seen.get(s, 0) < v:
                    handle.wait_ge(sems[s], v)
                    seen[s] = v
            ins = op.emit(handle)
            if op.signals:
                ins.then_inc(sems[op.sem], 16 if op.value and op.sem in self.dma_count else 1)


class Bank:
    def __init__(self, t):
        self.t, self.free = t, []


class Ring:

    def __init__(self, items):
        self.items, self.n = items, 0

    def get(self):
        b = self.items[self.n % len(self.items)]
        self.n += 1
        return b


def build_program(nc, x_in, wstream, gains, const_in, par_in, out, cat, pat, plan, stop=None):
    Q = Queues()
    pe = lambda f, *w: Q.put("pe", f, *w)
    act = lambda f, *w: Q.put("act", f, *w)
    dve = lambda f, *w: Q.put("dve", f, *w)
    pool = lambda f, *w: Q.put("pool", f, *w)

    with ExitStack() as ctx:
        def sb(name, cols, dt=F32, parts=P):
            return ctx.enter_context(nc.sbuf_tensor(name, [parts, cols], dt))

        raw = sb("raw", NRAW * TW)
        whi = sb("whi", NSPL * TW, F32R)
        wlo = sb("wlo", NSPL * TW, F32R)
        x = sb("x", 2 * D)
        hhi = sb("hhi", KD * S, F32R)
        hlo = sb("hlo", KD * S, F32R)
        gain = sb("gain", D)
        cst = sb("cst", cat["pool"][0])
        par = sb("par", par_in.shape[1])
        hid = [sb(f"hid{i}", 2 * S, F32R) for i in range(3)]
        sil = [sb(f"sil{i}", S) for i in range(2)]
        prod = [sb(f"prod{i}", S) for i in range(2)]
        gates = sb("gates", KD * 2 * S)
        arena = sb("arena", 12832)
        yhi = sb("yhi", 8 * S, F32R)
        ylo = sb("ylo", 8 * S, F32R)
        small = sb("small", 592)
        banks = [Bank(ctx.enter_context(nc.psum_tensor(f"bank{i}", [P, 512], F32))) for i in range(8)]
        work = Ring(banks[0:4])
        side = banks[4:8]

        C = lambda name: cst[:, cat[name][0]:cat[name][1]]
        PR = lambda name: par[:, pat[name][0]:pat[name][1]]
        ident = C("ident")

        ld_x = Q.dma("ld_x", lambda e: e.dma_start(x[:, :].rearrange("p (a n) -> p a n", a=2),
                                                   x_in.rearrange("(a p) n -> p a n", p=P)))
        gain_free = [[]]
        gain_no = [0]

        def load_gain():
            i = gain_no[0]
            gain_no[0] += 1
            return Q.dma("ld_gain", lambda e: e.dma_start(gain[:, :], gains[i]), *gain_free[0])

        ld_g = [load_gain()]
        ld_c = Q.dma("ld_c", lambda e: e.dma_start(cst[:, :], const_in[:, 0:cat["pool"][0]]))

        mhalf = small[:, 160:176]
        mh = pool(lambda e: e.memset(mhalf, -0.5))

        def rsqrt(out_, in_, eps, *ready):
            n = out_.shape[1]
            o = pool(lambda e: e.tensor_scalar(out_, in_, eps, None, ALU.add), *ready)
            return pool(lambda e: e.tensor_tensor(out_, out_, mhalf[:, 0:n], ALU.pow), o, mh)

        class Tile:
            pass

        tiles = []
        raw_free = [[] for _ in range(NRAW)]
        spl_free = [None] * NSPL
        state = {"dma": 0, "split": 0, "next": 0}

        def issue_dma():
            j = state["dma"]
            if j >= len(plan):
                return
            name, n, split, off = plan[j]
            t = Tile()
            t.name, t.n, t.split, t.slot = name, n, split, j % NRAW
            t.raw = raw[:, t.slot * TW:t.slot * TW + n]
            t.load = Q.dma(f"raw{t.slot}", lambda e, t=t, off=off, n=n: e.dma_start(t.raw, wstream[off * P:(off + n) * P].rearrange("(p n) -> p n", p=P)),
                           *raw_free[t.slot])
            raw_free[t.slot] = None
            tiles.append(t)
            state["dma"] += 1

        def issue_split():
            j = state["split"]
            if j >= len(plan):
                return
            while state["dma"] <= j:
                issue_dma()
            t = tiles[j]
            state["split"] += 1
            if not t.split:
                t.ready = [t.load]
                return
            s, n = j % NSPL, t.n
            t.hi, t.lo = whi[:, s * TW:s * TW + n], wlo[:, s * TW:s * TW + n]
            prior = [spl_free[s]] if spl_free[s] is not None else []
            hi = act(lambda e: e.activation(t.hi, t.raw, ACT.Copy), t.load, *prior)
            lo = dve(lambda e: e.tensor_tensor(t.lo, t.raw, t.hi.bitcast(F32), ALU.subtract), hi)
            t.spl = s
            raw_free[t.slot] = [lo]
            t.ready = [hi, lo]
            issue_dma_upto(j + NRAW)

        def issue_dma_upto(j):
            while state["dma"] <= min(j, len(plan) - 1) and raw_free[state["dma"] % NRAW] is not None:
                issue_dma()

        def next_tile(name):
            j = state["next"]
            state["next"] += 1
            while state["split"] <= min(j + AHEAD, len(plan) - 1):
                issue_split()
            t = tiles[j]
            assert t.name == name, (t.name, name)
            return t

        def release(t, mm):
            if t.split:
                spl_free[t.spl] = mm
            else:
                raw_free[t.slot] = [mm]
                issue_dma_upto(state["next"] - 1 + NRAW)

        issue_dma_upto(1)
        ld_p = Q.dma("ld_p", lambda e: e.dma_start(par[:, :], par_in))
        issue_dma_upto(NRAW - 1)

        def mm3(psum, shi, slo, mhi, mlo, first, last, waits=()):
            pe(lambda e: e.matmul(psum, shi, mhi, start=first, stop=False, skip_group_check=True), *waits)
            pe(lambda e: e.matmul(psum, shi, mlo, start=False, stop=False, skip_group_check=True))
            return pe(lambda e: e.matmul(psum, slo, mhi, start=False, stop=last, skip_group_check=True))

        H = {"ready": [], "readers": []}

        def hT(buf, k, a=0, b=S):
            return buf[:, k * S + a:k * S + b]

        def feat_block(name, psum, first_waits, start, nk=KD, hi=hhi, lo=hlo, ready=None, part=0, t=None):
            t = t or next_tile(name)
            ready = H["ready"] if ready is None else ready
            for k in range(nk):
                w = (part * nk + k) * P
                mm = mm3(psum, t.hi[:, w:w + P], t.lo[:, w:w + P], hT(hi, k), hT(lo, k),
                         start and k == 0, k == nk - 1, (t.ready, first_waits, ready) if k == 0 else ())
            release(t, mm)
            return mm

        def tok_group(tag, n, tick=None):
            b = [work.get(), work.get()]
            fin = [None, None]
            for k0, m in a_group(n):
                t = next_tile(f"{tag}{k0}")
                for a in range(2):
                    for k in range(k0, k0 + m):
                        mv = (k - k0) * n
                        fin[a] = mm3(b[a].t[:, 0:n], hT(hhi, k, a * P, a * P + P), hT(hlo, k, a * P, a * P + P),
                                     t.hi[:, mv:mv + n], t.lo[:, mv:mv + n], k == 0, k == KD - 1,
                                     (t.ready, H["ready"], b[a].free) if k == k0 else ())
                release(t, fin[1])
                if tick:
                    tick()
            H["readers"] = [fin[1]]
            return b, fin

        def accum_block(name, shi, slo, ready, first, last, t=None):
            t = t or next_tile(name)
            for a in range(2):
                for h in range(2):
                    mm = mm3(side[2 * a + h].t[:, :], shi[:, a * P:a * P + P], slo[:, a * P:a * P + P],
                             t.hi[:, h * 512:h * 512 + 512], t.lo[:, h * 512:h * 512 + 512], first, last,
                             (t.ready, ready, side[2 * a + h].free) if (a, h) == (0, 0) or first else ())
                    if last:
                        acc_done[2 * a + h] = mm
            release(t, mm)
            return mm

        acc_done = [None] * 4
        st = small[:, 0:8]
        junk = [arena[:, 0:1024], arena[:, 1024:2048]]

        def residual(scale):
            ops = []
            for a in range(2):
                row = []
                for h in range(2):
                    o = x[:, a * D + h * 512:a * D + h * 512 + 512]
                    b = side[2 * a + h]
                    op = dve(lambda e, o=o, b=b: e.scalar_tensor_tensor(o, b.t[:, :], scale, o, ALU.mult, ALU.add),
                             acc_done[2 * a + h])
                    b.free = [op]
                    row.append(op)
                ops.append(row)
            return ops

        arena_free = [[]]

        def norm(x_ready):
            fin = []
            for a in range(2):
                xa = x[:, a * D:a * D + D]
                sq = act(lambda e, a=a, xa=xa: e.activation(junk[0], xa, ACT.Square, scale=1.0 / 32,
                                                            accum_out=st[:, a:a + 1]), x_ready[a], arena_free[0])
                rs = rsqrt(st[:, 2 + a:3 + a], st[:, a:a + 1], EPS, sq)
                xn = dve(lambda e, a=a, xa=xa: e.scalar_tensor_tensor(junk[1], xa, st[:, 2 + a:3 + a], gain[:, :],
                                                                      ALU.mult, ALU.mult), rs, ld_g[0], arena_free[0],
                         fin[-1:] and [tr])
                for g in range(2):
                    b = work.get()
                    for k in range(4):
                        kk = 4 * g + k
                        tr = pe(lambda e, b=b, k=k, kk=kk: e.transpose(b.t[:, k * P:k * P + P], junk[1][:, kk * P:kk * P + P], ident),
                                xn, b.free, ld_c)
                    dst = lambda buf, a=a, g=g: buf[:, :].rearrange("p (k t) -> p k t", t=S)[:, 4 * g:4 * g + 4, a * P:a * P + P]
                    src = b.t[:, :].rearrange("p (k t) -> p k t", t=P)
                    hi = act(lambda e, dst=dst, src=src: e.activation(dst(hhi), src, ACT.Copy), tr, H["readers"])
                    lo = dve(lambda e, dst=dst, src=src: e.tensor_tensor(dst(hlo), src, dst(hhi).bitcast(F32), ALU.subtract), hi)
                    b.free = [lo]
                    fin.append(lo)
            H["ready"] = fin
            gain_free[0] = [xn]
            if gain_no[0] < 8:
                ld_g[0] = load_gain()
            arena_free[0] = [tr]

        hid_ring = Ring([Bank(h) for h in hid])
        sil_ring = Ring([Bank(h) for h in sil])
        prod_ring = Ring([Bank(h) for h in prod])

        def split_hidden(src, src_ready, extra=()):
            hb = hid_ring.get()
            hi = act(lambda e: e.activation(hb.t[:, 0:S], src, ACT.Copy), src_ready, hb.free)
            lo = dve(lambda e: e.tensor_tensor(hb.t[:, S:2 * S], src, hb.t[:, 0:S].bitcast(F32), ALU.subtract), hi)
            return hb, lo

        def ffn(tag, hidden_fn, scale):
            pend = {}
            for i in range(NF + 2):
                if i < NF:
                    b = work.get()
                    feat_block(f"{tag}a{i}", b.t[:, 0:S], b.free, True)
                    up = feat_block(f"{tag}b{i}", b.t[:, S:2 * S], (), False)
                    pend[i] = hidden_fn(i, b, up)
                if i >= 2:
                    hb, ready = pend.pop(i - 2)
                    mm = accum_block(f"{tag}d{i - 2}", hb.t[:, 0:S], hb.t[:, S:2 * S], ready, i == 2, i == NF + 1)
                    hb.free = [mm]
            H["readers"] = [up]
            return residual(scale)

        def swiglu_hidden(i, b, up):
            s, p = sil_ring.get(), prod_ring.get()
            a1 = act(lambda e: e.activation(s.t[:, :], b.t[:, 0:S], ACT.Silu), up, s.free)
            m1 = dve(lambda e: e.tensor_tensor(p.t[:, :], s.t[:, :], b.t[:, S:2 * S], ALU.mult), a1, p.free)
            b.free, s.free = [m1], [m1]
            hb, lo = split_hidden(p.t[:, :], m1)
            p.free = [lo]
            return hb, lo

        def gate_block(tag, f, bias):
            b = work.get()
            for j in range(2):
                mm = feat_block(f"{tag}g{j}{f}", b.t[:, j * S:j * S + S], b.free if j == 0 else (), j == 0)
                yield mm
            ops = []
            for j in range(2):
                g = gates[:, (2 * f + j) * S:(2 * f + j + 1) * S]
                ops.append(act(lambda e, g=g, j=j: e.activation(g, b.t[:, j * S:j * S + S], ACT.Tanh, scale=0.5,
                                                                bias=bias[:, j * KD + f:j * KD + f + 1]), mm, halfb[0], gates_free[0]))
            b.free = ops
            gate_ops[f] = ops

        gate_ops = {}
        halfb = [None]

        def merge_tail(tag, y_ready):
            pend = {}
            for i in range(KD + 1):
                if i < KD:
                    b = work.get()
                    t = next_tile(f"{tag}br{i}")
                    feat_block(None, b.t[:, 0:S], b.free, True, nk=4, hi=yhi, lo=ylo, ready=y_ready, part=0, t=t)
                    mm = feat_block(None, b.t[:, S:2 * S], (), False, nk=4, hi=yhi[:, 4 * S:8 * S], lo=ylo[:, 4 * S:8 * S],
                                    ready=y_ready, part=1, t=t)
                    s, p = sil_ring.get(), prod_ring.get()
                    g = [gates[:, (2 * i + j) * S:(2 * i + j + 1) * S] for j in range(2)]
                    m0 = dve(lambda e, s=s, g=g, b=b: e.scalar_tensor_tensor(s.t[:, :], g[0], 1.0, b.t[:, 0:S], ALU.add, ALU.mult),
                             mm, gate_ops[i], s.free)
                    m1 = dve(lambda e, p=p, g=g, b=b: e.scalar_tensor_tensor(p.t[:, :], g[1], 1.0, b.t[:, S:2 * S], ALU.add, ALU.mult),
                             p.free)
                    m2 = dve(lambda e, s=s, p=p: e.tensor_tensor(p.t[:, :], s.t[:, :], p.t[:, :], ALU.add), m0, m1)
                    b.free, s.free = [m1], [m2]
                    hb, lo = split_hidden(p.t[:, :], m2)
                    p.free = [lo]
                    pend[i] = (hb, lo)
                if i >= 1:
                    hb, ready = pend.pop(i - 1)
                    m = accum_block(f"{tag}wo{i - 1}", hb.t[:, 0:S], hb.t[:, S:2 * S], ready, i == 1, i == KD)
                    hb.free = [m]
            return mm, residual(0.5)

        A = {}

        def region(name, off, n):
            A[name] = arena[:, off:off + n]
            return A[name]

        def v3d(ap, b, c):
            return ap.rearrange("p (b c) -> p b c", b=b, c=c)

        def rope_tables(dst, w, nk, waits):
            ops = []
            for a in range(2):
                for k in range(nk):
                    wk = w[:, k * 64:k * 64 + 64]
                    c = dst[:, (a * nk + k) * 64:(a * nk + k + 1) * 64]
                    s = dst[:, ((2 + a) * nk + k) * 64:((2 + a) * nk + k + 1) * 64]
                    cs, sn = C("cos")[:, a * 64:a * 64 + 64], C("sin")[:, a * 64:a * 64 + 64]
                    ops.append(pool(lambda e, c=c, cs=cs, wk=wk: e.tensor_tensor(c, cs, wk, ALU.mult), *waits, ld_c, ld_p))
                    ops.append(pool(lambda e, s=s, sn=sn, wk=wk: e.tensor_tensor(s[:, 0:32], sn[:, 0:32], wk[:, 32:64], ALU.mult)))
                    ops.append(pool(lambda e, s=s, sn=sn, wk=wk: e.tensor_tensor(s[:, 32:64], sn[:, 32:64], wk[:, 0:32], ALU.mult)))
            return ops[-1]

        def rope(src, tab, a, nh, nk, tmp, dst, tab_ready, waits):
            per = nh // nk
            sv = src.rearrange("p (k h d) -> p k h d", k=nk, d=64)
            tv = tmp.rearrange("p (k h d) -> p k h d", k=nk, d=64)
            dv = dst.rearrange("p (k h d) -> p k h d", k=nk, d=64)
            o = None
            for k in range(nk):
                cb = tab[:, (a * nk + k) * 64:(a * nk + k) * 64 + 64]
                sn = tab[:, ((2 + a) * nk + k) * 64:((2 + a) * nk + k) * 64 + 64]
                cbb = cb.rearrange("p (o d) -> p o d", o=1).to_broadcast([P, per, 64])
                s1 = sn[:, 0:32].rearrange("p (o d) -> p o d", o=1).to_broadcast([P, per, 32])
                s2 = sn[:, 32:64].rearrange("p (o d) -> p o d", o=1).to_broadcast([P, per, 32])
                m1 = pool(lambda e, k=k, s1=s1: e.tensor_tensor(tv[:, k, :, 0:32], sv[:, k, :, 32:64], s1, ALU.mult), waits, tab_ready)
                m2 = pool(lambda e, k=k, s2=s2: e.tensor_tensor(tv[:, k, :, 32:64], sv[:, k, :, 0:32], s2, ALU.mult))
                m3 = dve(lambda e, k=k, cbb=cbb: e.tensor_tensor(dv[:, k], sv[:, k], cbb, ALU.mult), waits, tab_ready)
                o = dve(lambda e, k=k: e.tensor_tensor(dv[:, k], dv[:, k], tv[:, k], ALU.add), m2, m3)
            return o

        def head_stats(src, nh, sqbuf, out8, waits, post=None):
            sq = act(lambda e: e.activation(sqbuf, src, ACT.Square, scale=0.125), *waits)
            rd = dve(lambda e: e.tensor_reduce(out8, sqbuf.rearrange("p (h d) -> p h d", d=64), AX, ALU.add), sq)
            return sq, rsqrt(out8, out8, EPS, rd)

        def transpose4(bank, srcs, ready, dst, dst_free):
            for k, s in enumerate(srcs):
                tr = pe(lambda e, k=k, s=s: e.transpose(bank.t[:, k * P:k * P + P], s, ident), ready, bank.free, ld_c)
            ev = act(lambda e: e.activation(dst, bank.t[:, 0:P * len(srcs)].rearrange("p (k t) -> p k t", t=P), ACT.Copy), tr, dst_free)
            bank.free = [ev]
            return ev, tr

        def softmax_heads(jobs, qk_ready, sc, nsc, vpad_ready, y_out, p_first=None):
            n = len(jobs)
            mem = {}
            for i in range(n + 2):
                if i < n:
                    J = jobs[i]
                    b = side[i % 2]
                    s1 = pe(lambda e, J=J, b=b: e.matmul(b.t[:, 0:P], J["q"](0, P), J["k"](0, P), start=True, stop=True), b.free, qk_ready)
                    s1 = pe(lambda e, J=J, b=b: e.matmul(b.t[:, P:3 * P], J["q"](P, S), J["k"](0, S), start=True, stop=True))
                    sm, nb, rr = smb[i % 2], small[:, 64 + 8 * (i % 2):64 + 8 * (i % 2) + 8], None
                    cm = C("cmask")
                    fr = smb_free[i % 2]
                    r0 = dve(lambda e, b=b, sm=sm, nb=nb: e.tensor_tensor_reduce(sm[:, 0:P], b.t[:, 0:P], cm[:, 0:P], 1.0, -3.0e38, ALU.add, ALU.max, nb[:, 0:1]), s1, fr)
                    r1 = dve(lambda e, b=b, sm=sm, nb=nb: e.tensor_tensor_reduce(sm[:, P:3 * P], b.t[:, P:3 * P], cm[:, P:3 * P], 1.0, -3.0e38, ALU.add, ALU.max, nb[:, 1:2]))
                    b.free = [r1]
                    n2 = dve(lambda e, J=J, nb=nb: e.tensor_tensor(nb[:, 2:4], nb[:, 0:2], J["nsc"], ALU.mult), r0, r1)
                    pb = pbuf[i % 2]
                    e0 = act(lambda e, J=J, sm=sm, nb=nb, pb=pb: e.activation(pb[:, 0:P], sm[:, 0:P], ACT.Exp, bias=nb[:, 2:3], scale=J["sc"][:, 0:1], accum_out=nb[:, 4:5]), n2, pbuf_free[i % 2])
                    e1 = act(lambda e, J=J, sm=sm, nb=nb, pb=pb: e.activation(pb[:, P:3 * P], sm[:, P:3 * P], ACT.Exp, bias=nb[:, 3:4], scale=J["sc"][:, 1:2], accum_out=nb[:, 5:6]))
                    rc = dve(lambda e, nb=nb: e.reciprocal(nb[:, 6:8], nb[:, 4:6]), e0, e1)
                    if J["gate"] is not None:
                        rc = dve(lambda e, J=J, nb=nb: e.tensor_tensor(nb[:, 6:8], nb[:, 6:8], J["gate"], ALU.mult), rc)
                    q0 = dve(lambda e, nb=nb, pb=pb: e.tensor_scalar(pb[:, 0:P], pb[:, 0:P], nb[:, 6:7], None, ALU.mult), rc)
                    q1 = dve(lambda e, nb=nb, pb=pb: e.tensor_scalar(pb[:, P:3 * P], pb[:, P:3 * P], nb[:, 7:8], None, ALU.mult))
                    smb_free[i % 2] = [q1]
                    mem[i] = (pb, [q0, q1])
                    yield
                if 0 <= i - 1 < n:
                    pb, rdy = mem[i - 1]
                    b = side[2]
                    for d, s in ((0, 0), (1, 1), (2, 2)):
                        tr = pe(lambda e, pb=pb, b=b, d=d: e.transpose(b.t[:, d * P:d * P + P], pb[:, d * P:d * P + P], ident), rdy, b.free)
                    pbuf_free[(i - 1) % 2] = [tr]
                    pt = ptb[(i - 1) % 2]
                    ev = act(lambda e, pt=pt, b=b: e.activation(pt[:, :], b.t[:, 0:3 * P], ACT.Copy), tr, ptb_free[(i - 1) % 2])
                    b.free = [ev]
                    mem[i - 1] = (pt, ev)
                    yield
                if 0 <= i - 2 < n:
                    J = jobs[i - 2]
                    pt, ev = mem.pop(i - 2)
                    b = side[3]
                    o = b.t[:, 0:S]
                    if J["first"] and J.get("pre"):
                        J["pre"](o, b)
                    m = pe(lambda e, J=J, pt=pt, o=o: e.matmul(o, J["v"](0), pt[:, 0:S], start=J["first"] and not J.get("pre"), stop=False, skip_group_check=True),
                           ev, b.free, vpad_ready)
                    m = pe(lambda e, J=J, pt=pt, o=o: e.matmul(o[:, P:S], J["v"](1), pt[:, S:3 * P], start=False, stop=J["last"], skip_group_check=True))
                    ptb_free[(i - 2) % 2] = [m]
                    if J["last"]:
                        y_out(J["pair"], b, m)
                    yield

        def split_y(blk, src, ready, wait_free):
            hi = act(lambda e: e.activation(yhi[:, blk * S:blk * S + S], src, ACT.Copy), ready, wait_free)
            lo = dve(lambda e: e.tensor_tensor(ylo[:, blk * S:blk * S + S], src, yhi[:, blk * S:blk * S + S].bitcast(F32), ALU.subtract), hi)
            return lo

        R = {}
        o_ = 0
        for nm, n in (("smb", 768), ("pbuf", 768), ("ptb", 768), ("qT", 1024), ("kT", 1024),
                      ("vpad", 2048), ("us", 1024), ("dT", 256), ("tab", 512), ("pool", 1536), ("pw", 512)):
            R[nm] = arena[:, o_:o_ + n]
            o_ += n
        for i, nm in enumerate(("ks", "qs", "tmp", "ro")):
            R[nm] = gates[:, i * 1024:i * 1024 + 1024]
        gates_free = [[]]
        smb = [R["smb"][:, 0:384], R["smb"][:, 384:768]]
        pbuf = [R["pbuf"][:, 0:384], R["pbuf"][:, 384:768]]
        ptb = [R["ptb"][:, 0:384], R["ptb"][:, 384:768]]
        smb_free, pbuf_free, ptb_free = [[], []], [[], []], [[], []]
        scq = small[:, 96:112]
        nscq = small[:, 112:128]
        rk = small[:, 128:144]
        hb16 = small[:, 144:160]
        Y = {"readers": []}

        def mixer1(l):
            T = f"L{l}"
            start = arena_free[0]
            halfb[0] = pool(lambda e: e.tensor_scalar(hb16, PR(f"bg{l}"), 0.5, None, ALU.mult), ld_p, *gate_ops.get(KD - 1, []))
            tabk, tabq = R["tab"][:, 0:256], R["tab"][:, 256:512]
            tk = rope_tables(tabk, PR(f"kn{l}"), 1, start)
            tq = rope_tables(tabq, PR(f"qn{l}"), 1, ())
            zv = pool(lambda e: e.memset(R["vpad"], 0.0), start)
            bg = []

            def tick(n=1):
                for _ in range(n):
                    while bg:
                        try:
                            next(bg[0])
                            break
                        except StopIteration:
                            bg.pop(0)

            def evac_qk(b, fin, dst, waits):
                ops = []
                for a in range(2):
                    ops.append(act(lambda e, a=a: e.activation(dst[:, a * 512:a * 512 + 512], b[a].t[:, :], ACT.Copy), fin[a], waits))
                    b[a].free = [ops[-1]]
                return ops

            res = {}

            def kq(nm, b, fin, tab, tabr, isq):
                src = R["qs"] if isq else R["ks"]
                ev = evac_qk(b, fin, src, start)
                for a in range(2):
                    sv = src[:, a * 512:a * 512 + 512]
                    tv = R["tmp"][:, (a * 512):(a * 512) + 512]
                    st8 = (scq if isq else rk)[:, a * 8:a * 8 + 8]
                    rv = R["ro"][:, a * 512:a * 512 + 512]
                    sq, rs = head_stats(sv, 8, rv, st8, (ev[a], res.get("tr", []), start))
                    if isq:
                        r1 = pool(lambda e, a=a, st8=st8: e.tensor_scalar(nscq[:, a * 8:a * 8 + 8], st8, -0.125, None, ALU.mult), rs, res.get("nsc", []))
                        r2 = pool(lambda e, st8=st8: e.tensor_scalar(st8, st8, 0.125, None, ALU.mult), r1)
                        pre = [r2, rs]
                        res["sc"] = r2
                    else:
                        rb = st8.rearrange("p (h o) -> p h o", o=1).to_broadcast([P, 8, 64])
                        sv3 = v3d(sv, 8, 64)
                        pre = [dve(lambda e, sv3=sv3, rb=rb: e.tensor_tensor(sv3, sv3, rb, ALU.mult), rs)]
                    ro = rope(sv, tab, a, 8, 1, tv, rv, tabr, (pre,))
                    yield
                    bank = side[a]
                    dT = (R["qT"] if isq else R["kT"]).rearrange("p (k t) -> p k t", t=S)[:, :, a * P:a * P + P]
                    evt, tr = transpose4(bank, [rv[:, c * P:c * P + P] for c in range(4)], ro, dT, start)
                    res.setdefault("trn", []).append(tr)
                    res[nm, a] = evt
                    yield
                res["tr"] = res.pop("trn")

            b, fin = tok_group(T + "k", 512)
            bg.append(kq("k", b, fin, tabk, tk, False))
            b, fin = tok_group(T + "q", 512, tick)
            bg.append(kq("q", b, fin, tabq, tq, True))
            b, fin = tok_group(T + "v", 512, tick)
            vops = []
            for a in range(2):
                dst = R["vpad"][:, a * 1024:a * 1024 + 1024].rearrange("p (c y) -> p c y", y=256)
                for j in range(2):
                    vops.append(act(lambda e, a=a, j=j, dst=dst, b=b: e.activation(dst[:, :, 192 * j:192 * j + 64],
                                    b[a].t[:, :].rearrange("p (c j d) -> p c j d", j=2, d=64)[:, :, j, :], ACT.Copy), fin[a], zv))
                b[a].free = [vops[-1]]
            b, fin = tok_group(T + "u", 512, tick)
            us = R["us"]
            uops = []
            for a in range(2):
                uops.append(act(lambda e, a=a, b=b: e.activation(us[:, a * 512:a * 512 + 512], b[a].t[:, :], ACT.Copy), fin[a], start))
                b[a].free = [uops[-1]]

            def poolers():
                fr = []
                for g in range(4):
                    bank = side[g % 2]
                    pm = R["pool"][:, g * 384:g * 384 + 384]
                    pe(lambda e, g=g, bank=bank, pm=pm: e.matmul(bank.t[:, 0:S], us[:, g * P:g * P + P], pm[:, 0:S], start=True, stop=False, skip_group_check=True),
                       uops, bank.free, pw_ld[0])
                    m = pe(lambda e, g=g, bank=bank, pm=pm: e.matmul(bank.t[:, P:S], us[:, 512 + g * P:512 + g * P + P], pm[:, S:S + P], start=False, stop=True, skip_group_check=True))
                    dT = R["dT"]
                    ev = act(lambda e, bank=bank: e.activation(dT, bank.t[:, 0:S], ACT.Copy), m, fr)
                    bank.free = [ev]
                    yield
                    bank = side[2 + g % 2]
                    m = pe(lambda e, g=g, bank=bank: e.matmul(bank.t[:, 0:S], pw[:, g * P:g * P + P], dT, start=True, stop=True), ev, bank.free, pw_ld[0])
                    fr = [m]
                    sc = PR(f"ps{l}")[:, g:g + 1]
                    dst = yhi[:, g * S:g * S + S]
                    hi = act(lambda e, g=g, bank=bank, sc=sc, dst=dst: e.activation(dst, bank.t[:, 0:S], ACT.Copy, scale=sc), m, Y["readers"])
                    lo = dve(lambda e, g=g, bank=bank, sc=sc, dst=dst: e.scalar_tensor_tensor(ylo[:, g * S:g * S + S], bank.t[:, 0:S], sc, dst.bitcast(F32), ALU.mult, ALU.subtract), hi)
                    bank.free = [lo]
                    res.setdefault("y", []).append(lo)
                    yield
                pw_free[0] = fr

            bg.append(poolers())
            def jobs():
                out_ = []
                for h in range(8):
                    c, o = h // 2, 64 * (h % 2)
                    out_.append(dict(
                        q=lambda a, b_, c=c, o=o: R["qT"][o:o + 64, c * S + a:c * S + b_],
                        k=lambda a, b_, c=c, o=o: R["kT"][o:o + 64, c * S + a:c * S + b_],
                        sc=scq.rearrange("p (a h) -> p h a", a=2)[:, h, :], nsc=nscq.rearrange("p (a h) -> p h a", a=2)[:, h, :],
                        v=lambda s, h=h: R["vpad"][:, s * 1024 + h * P:s * 1024 + h * P + P],
                        gate=None, pair=c, first=h % 2 == 0, last=h % 2 == 1))
                return out_

            def y_out(pair, b, m):
                lo = split_y(4 + pair, b.t[:, 0:S], m, Y["readers"])
                b.free = [lo]
                res["y"].append(lo)

            def attn():
                yield from softmax_heads(jobs(), [res["k", 0], res["k", 1], res["q", 0], res["q", 1], res["sc"]], scq, nscq, vops, y_out)
            bg.append(attn())
            gates_free[0] = [res["k", 0], res["k", 1], res["q", 0], res["q", 1]]
            for f in range(KD):
                for gmm in gate_block(T, f, hb16):
                    tick(2)
            while bg:
                tick()
            H["readers"] = [gmm]
            mm, xr = merge_tail(T, res["y"])
            Y["readers"] = [mm]
            arena_free[0] = [mm, res["y"][-1], gate_ops[KD - 1][1]]
            res_ops = xr
            return res_ops

        pw = R["pw"]
        pw_free = [[]]
        pw_ld = [None]

        def load_pool_w(l):
            pw_ld[0] = [Q.dma("ld_pw", lambda e: e.dma_start(pw, par_dram_pw[l]), pw_free[0], arena_free[0]),
                        Q.dma("ld_pm", lambda e: e.dma_start(R["pool"], const_in[:, cat["pool"][0]:cat["pool"][1]]))]

        def mixer2():
            start = [arena_free[0]]
            a0 = lambda lo_, n: arena[:, lo_:lo_ + n]
            kraw, qraw, tmpb, rob = R["ks"], R["qs"], R["tmp"], R["ro"]
            qT, kT, vp, mqk, qkT = a0(2304, 1024), a0(3328, 1024), a0(4352, 1536), a0(5888, 1040), a0(6928, 1024)
            tab, mv, gmo = a0(7952, 1024), a0(8976, 1040), a0(10016, 1024)
            kc2, vc2, X = a0(11040, 512), a0(11552, 512), [kraw[:, 0:480], kraw[:, 480:960]]
            hm = a0(11040, 1024)
            Eb = [a0(12064, 384), a0(12448, 384)]
            Pb = [mqk[:, 0:384], mqk[:, 384:768]]
            Vb, Pc, PcT = tab[:, 0:512], tab[:, 512:768], tab[:, 768:1024]
            w16 = small[:, 176:192]
            gt = small[:, 192:240]
            ifs = small[:, 240:256]
            hc = small[:, 256:376]
            kcT = small[:, 376:406]
            vcs = small[0:15, 408:536]
            acol, ecol = small[:, 536:544], small[:, 544:552]
            ms = small[:, 552:560]
            dcol = small[:, 560:576]
            mx16 = small[:, 576:592]
            rows = [prod[0], prod[1], sil[0], sil[1]]
            row = lambda i: rows[i][0:4, :]
            halfb[0] = pool(lambda e: e.tensor_scalar(hb16, PR("mg"), 0.5, None, ALU.mult), ld_p, *gate_ops[KD - 1])
            tabk, tabq = tab[:, 0:768], tab[:, 768:1024]
            tk = rope_tables(tabk, PR("kn3"), 3, start)
            tq = rope_tables(tabq, PR("qn2"), 1, ())
            z1 = pool(lambda e: e.memset(vp, 0.0), start)
            z2 = pool(lambda e: e.memset(mqk, 0.0), start)
            z3 = pool(lambda e: e.memset(mv, 1.0), start)
            bg, bg2 = [], []
            res = {"y": []}

            def tick(n=1):
                for _ in range(n):
                    for lst in (bg, bg2):
                        while lst:
                            try:
                                next(lst[0])
                                break
                            except StopIteration:
                                lst.pop(0)

            b, fin = tok_group("Mk3", 512)
            kev = []
            for a in range(2):
                kev.append(act(lambda e, a=a, b=b: e.activation(kraw[:, a * 512:a * 512 + 512], b[a].t[:, :], ACT.Copy), fin[a], start))
                b[a].free = [kev[-1]]

            def kproc():
                for a in range(2):
                    sv = kraw[:, a * 512:a * 512 + 384]
                    st6 = rk[:, a * 8:a * 8 + 6]
                    rv = rob[:, a * 512:a * 512 + 384]
                    sq, rs = head_stats(sv, 6, rv, st6, (kev[a], start))
                    rb = st6.rearrange("p (h o) -> p h o", o=1).to_broadcast([P, 6, 64])
                    sv3 = v3d(sv, 6, 64)
                    nr = dve(lambda e, sv3=sv3, rb=rb: e.tensor_tensor(sv3, sv3, rb, ALU.mult), rs)
                    ro = rope(sv, tabk, a, 6, 3, tmpb[:, a * 512:a * 512 + 384], rv, tk, ([nr],))
                    yield
                    bank = side[a]
                    dup = a0(a * 1024, 1024)
                    dv = dup.rearrange("p (h o d) -> p h o d", o=2, d=64)
                    d1 = pool(lambda e, dv=dv, rv=rv: e.tensor_copy(dv[:, 0:6], rv.rearrange("p (h o d) -> p h o d", o=1, d=64).to_broadcast([P, 6, 2, 64])), ro, start)
                    d2 = pool(lambda e, dv=dv, a=a: e.tensor_copy(dv[:, 6:8], kraw[:, a * 512 + 384:a * 512 + 512].rearrange("p (h o d) -> p h o d", o=1, d=64).to_broadcast([P, 2, 2, 64])))
                    for i in range(4):
                        tr = pe(lambda e, i=i, dup=dup, bank=bank: e.transpose(bank.t[:, i * P:i * P + P], dup[:, (2 + i) * P:(3 + i) * P], ident), d1, bank.free)
                    dst = kT.rearrange("p (k t) -> p k t", t=S)[:, :, a * P:a * P + P]
                    ev = act(lambda e, dst=dst, bank=bank: e.activation(dst, bank.t[:, :].rearrange("p (k t) -> p k t", t=P), ACT.Copy), tr, start)
                    bank.free = [ev]
                    res["kT", a] = ev
                    yield
                    for i in range(4):
                        j = i if i < 2 else i + 4
                        tr = pe(lambda e, i=i, j=j, dup=dup, bank=bank: e.transpose(bank.t[:, i * P:i * P + P], dup[:, j * P:j * P + P], ident), d2, bank.free)
                    bv = bank.t[:, :].rearrange("p (k g t) -> p k g t", k=2, g=2)
                    ops = []
                    for k, buf in enumerate((kc2, vc2)):
                        bb = buf.rearrange("p (g t) -> p g t", g=2)
                        s0 = 1 - a
                        ops.append(act(lambda e, bb=bb, k=k, a=a, bv=bv: e.activation(bb[0:64, :, a * P:a * P + P], bv[0:64, k], ACT.Copy), tr, start))
                        ops.append(act(lambda e, bb=bb, k=k, a=a, s0=s0, bv=bv: e.activation(bb[64:P, :, a * P - 1 + s0:a * P + P - 1], bv[64:P, k, :, s0:P], ACT.Copy)))
                    bank.free = ops[-1:]
                    res["c2", a] = ops
                    res.setdefault("ktr", []).append(d1)
                    yield
                for k, (buf, pn) in enumerate(((kc2, "kpe"), (vc2, "vpe"))):
                    xv = X[k].rearrange("p (j g n) -> p j g n", j=16, g=2)
                    for g in range(2):
                        for jh in range(2):
                            in0 = buf[:, g * S:g * S + S].rearrange("p (n j two) -> p j n two", j=8, two=2)[:, :, jh:jh + 15, 0]
                            pb_ = PR(pn)[:, 8 * jh:8 * jh + 8].rearrange("p (j o) -> p j o", o=1).to_broadcast([P, 8, 15])
                            o = pool(lambda e, xv=xv, g=g, jh=jh, in0=in0, pb_=pb_: e.tensor_tensor(xv[:, 8 * jh:8 * jh + 8, g, :], in0, pb_, ALU.add),
                                     res["c2", 0], res["c2", 1], start, ld_p)
                res["X"] = o
                yield

            bg.append(kproc())
            b, fin = tok_group("Mv3", 288, tick)
            vops, gops = [], []
            for a in range(2):
                dst = vp.rearrange("p (k s g y) -> p k s g y", k=2, s=2, g=2)[:, :, a, :, 64:128]
                vops.append(act(lambda e, a=a, b=b, dst=dst: e.activation(dst, b[a].t[:, 0:256].rearrange("p (k g d) -> p k g d", k=2, g=2), ACT.Copy), fin[a], z1))
                i1 = act(lambda e, a=a, b=b: e.activation(ifs[:, a * 8:a * 8 + 8], b[a].t[:, 256:264], ACT.Copy))
                i2 = act(lambda e, a=a, b=b: e.activation(gt[:, a * 24:a * 24 + 24], b[a].t[:, 264:288], ACT.Tanh, scale=0.5))
                b[a].free = [i2]
                gops += [i1, i2]
            gfin = dve(lambda e: e.tensor_scalar(gt, gt, 0.5, 0.5, ALU.mult, ALU.add), gops)

            def lstm_rows():
                bank = side[2]
                for j in range(2):
                    for a in range(2):
                        m = pe(lambda e, j=j, a=a: e.matmul(bank.t[0:4, j * S + a * P:j * S + a * P + P], ifs[:, a * 8 + 4 * j:a * 8 + 4 * j + 4], ident, start=True, stop=True),
                               gops, bank.free)
                r1 = dve(lambda e: e.tensor_scalar(row(0), bank.t[0:4, 0:S], PR("ib")[0:4, :], None, ALU.add), m, ld_p)
                r2 = dve(lambda e: e.tensor_scalar(row(1), bank.t[0:4, S:2 * S], PR("fb")[0:4, :], None, ALU.add))
                bank.free = [r2]
                r3 = act(lambda e: e.activation(row(2), row(1), ACT.Abs), r2)
                r4 = act(lambda e: e.activation(row(2), row(2), ACT.Exp, scale=-1.0), r3)
                r5 = act(lambda e: e.activation(row(2), row(2), ACT.Ln, bias=1.0), r4)
                r6 = dve(lambda e: e.scalar_tensor_tensor(row(1), row(1), 0.0, row(2), ALU.min, ALU.subtract), r5)
                r7 = dve(lambda e: e.memset(row(3), 0.0))
                r8 = dve(lambda e: e.tensor_tensor_scan(row(2), row(1), row(3), 0.0, ALU.add, ALU.add), r6, r7)
                r9 = dve(lambda e: e.tensor_tensor(row(0), row(0), row(2), ALU.subtract), r8, r1)
                r10 = dve(lambda e: e.tensor_tensor_scan(row(1), row(0), row(0), 0.0, ALU.max, ALU.max), r9)
                r11 = dve(lambda e: e.tensor_tensor(row(3), row(2), row(1), ALU.add), r10)
                r12 = act(lambda e: e.activation(row(3), row(3), ACT.Exp, scale=-1.0), r11)
                yield
                for a in range(2):
                    pe(lambda e, a=a: e.matmul(bank.t[:, a * 4:a * 4 + 4], rows[0][0:4, a * P:a * P + P], ident[0:4, 0:4], start=True, stop=True), bank.free, r9)
                    m = pe(lambda e, a=a: e.matmul(bank.t[:, 8 + a * 4:12 + a * 4], rows[3][0:4, a * P:a * P + P], ident[0:4, 0:4], start=True, stop=True), r12)
                e1 = dve(lambda e: e.tensor_copy(small[:, 536:552], bank.t[:, 0:16]), m)
                bank.free = [e1]
                res["cols"], res["M"] = e1, r10
                yield

            bg.append(lstm_rows())
            b, fin = tok_group("Mnq", 512, tick)
            qev = []
            for a in range(2):
                qev.append(act(lambda e, a=a, b=b: e.activation(qraw[:, a * 512:a * 512 + 512], b[a].t[:, :], ACT.Copy), fin[a], start))
                b[a].free = [qev[-1]]

            def qproc():
                for a in range(2):
                    sv = qraw[:, a * 512:a * 512 + 512]
                    st8 = scq[:, a * 8:a * 8 + 8]
                    rv = rob[:, a * 512:a * 512 + 512]
                    sq, rs = head_stats(sv, 8, rv, st8, (qev[a], res["ktr"]))
                    r1 = pool(lambda e, a=a, st8=st8: e.tensor_scalar(nscq[:, a * 8:a * 8 + 8], st8, -0.125, None, ALU.mult), rs)
                    r2 = pool(lambda e, st8=st8: e.tensor_scalar(st8, st8, 0.125, None, ALU.mult), r1)
                    res["sc"] = r2
                    ro = rope(sv, tabq, a, 8, 1, tmpb[:, a * 512:a * 512 + 512], rv, tq, ([r2, sq],))
                    yield
                    dT = qT.rearrange("p (k t) -> p k t", t=S)[:, :, a * P:a * P + P]
                    evt, tr = transpose4(side[a], [rv[:, c * P:c * P + P] for c in range(4)], ro, dT, start)
                    res["qT", a] = evt
                    yield

            bg.append(qproc())
            cw, cb = PR("cw"), PR("cb")
            convs = []
            for f in range(4):
                bk = work.get()
                mm = feat_block(f"Mqk{f}", bk.t[:, 0:S], bk.free, True)
                xp = mqk[:, f * 260:f * 260 + 260]
                o = qkT[:, f * S:f * S + S]
                ev = act(lambda e, xp=xp, bk=bk: e.activation(xp[:, 3:259], bk.t[:, 0:S], ACT.Copy), mm, z2)
                bk.free = [ev]
                c0 = dve(lambda e, xp=xp, o=o, f=f: e.tensor_scalar(o, xp[:, 0:S], cw[:, 4 * f:4 * f + 1], cb[:, f:f + 1], ALU.mult, ALU.add), ev, ld_p, start)
                for k in range(1, 4):
                    c0 = dve(lambda e, xp=xp, o=o, f=f, k=k: e.scalar_tensor_tensor(o, xp[:, k:k + S], cw[:, 4 * f + k:4 * f + k + 1], o, ALU.mult, ALU.add), c0)
                th = Eb[f % 2][:, 0:S]
                t1 = act(lambda e, o=o, th=th: e.activation(th, o, ACT.Tanh, scale=0.5), c0, start, convs[-2:-1])
                convs.append(dve(lambda e, o=o, th=th: e.scalar_tensor_tensor(o, th, 1.0, o, ALU.add, ALU.mult), t1))
                tick()

            cbank = side[3]
            w1n = [0]

            def compress_step():
                i = w1n[0]
                w1n[0] += 1
                kv, q = i // 4, i % 4
                t = next_tile(f"M{'kv'[kv]}w1{q}")
                for jj in range(4):
                    j = 4 * q + jj
                    for hb_ in range(2):
                        o = cbank.t[:, (kv * 2 + hb_) * 30:(kv * 2 + hb_) * 30 + 30]
                        mm = pe(lambda e, o=o, t=t, jj=jj, hb_=hb_, j=j, kv=kv, i=i: e.matmul(
                                o, t.raw[:, jj * 256 + hb_ * P:jj * 256 + hb_ * P + P], X[kv][:, j * 30:j * 30 + 30],
                                start=(i == 0 and jj == 0 and hb_ == 0), stop=(j == 15), skip_group_check=True),
                                t.ready, res["X"], cbank.free if i == 0 else [])
                release(t, mm)
                res["cmp"] = mm

            def step():
                tick()
                compress_step()

            def compressed():
                g1 = act(lambda e: e.activation(hc, cbank.t[:, 0:120], ACT.Gelu), res["cmp"])
                cbank.free = [g1]
                bank = side[2]
                for hb_ in range(2):
                    m = pe(lambda e, hb_=hb_: e.matmul(bank.t[:, 0:30], PR("kw2")[:, hb_ * P:hb_ * P + P], hc[:, hb_ * 30:hb_ * 30 + 30], start=hb_ == 0, stop=hb_ == 1),
                           g1, bank.free, ld_p)
                for g in range(2):
                    for hb_ in range(2):
                        m = pe(lambda e, hb_=hb_, g=g: e.matmul(bank.t[0:15, 64 + g * 64:128 + g * 64], hc[:, (2 + hb_) * 30 + g * 15:(2 + hb_) * 30 + g * 15 + 15],
                                                                PR("vw2")[:, hb_ * P:hb_ * P + 64], start=hb_ == 0, stop=hb_ == 1))
                e1 = act(lambda e: e.activation(kcT, bank.t[:, 0:30], ACT.Copy), m)
                e2 = act(lambda e: e.activation(vcs, bank.t[0:15, 64:192], ACT.Copy))
                bank.free = [e2]
                yield
                bank = side[3]
                for g in range(2):
                    m = pe(lambda e, g=g, bank=bank: e.matmul(bank.t[:, 256:320], C("rep")[0:15, g * P:g * P + P], vcs[:, g * 64:g * 64 + 64], start=g == 0, stop=g == 1), e2, bank.free)
                e3 = dve(lambda e, bank=bank: e.tensor_tensor(Vb.rearrange("p (b d) -> p b d", d=64), bank.t[:, 256:320].rearrange("p (o d) -> p o d", o=1).to_broadcast([P, 8, 64]),
                                                   C("bd").rearrange("p (b d) -> p b d", d=64), ALU.mult), m, res["kdone"])
                bank.free = [e3]
                cbk = [side[2], side[0]]
                for a in range(2):
                    for h in range(8):
                        c, o, g = h // 2, 64 * (h % 2), h // 4
                        bank = cbk[h % 2]
                        m = pe(lambda e, a=a, h=h, c=c, o=o, g=g, bank=bank: e.matmul(bank.t[:, (a * 8 + h) * 16:(a * 8 + h) * 16 + 15], qT[o:o + 64, c * S + a * P:c * S + a * P + P],
                                kcT[o:o + 64, g * 15:g * 15 + 15], start=True, stop=True), e1, bank.free, [res["qT", 0], res["qT", 1]])
                zc = pool(lambda e: e.memset(Pc, 0.0), res["cmp"], res["kdone"])
                p3 = Pc.rearrange("p (r n) -> p r n", n=16)[:, :, 0:15]
                bc = lambda v: v.rearrange("p (r o) -> p r o", o=1).to_broadcast([P, 16, 15])
                for par_ in range(2):
                    s3 = cbk[par_].t[:, 0:256].rearrange("p (r two n) -> p two r n", n=16, two=2)[:, par_, :, 0:15]
                    pp = Pc.rearrange("p (r two n) -> p two r n", n=16, two=2)[:, par_, :, 0:15]
                    sq_ = scq.rearrange("p (r two) -> p two r", two=2)[:, par_, :]
                    c1 = dve(lambda e, pp=pp, s3=s3, sq_=sq_: e.tensor_tensor(pp, s3, sq_.rearrange("p (r o) -> p r o", o=1).to_broadcast([P, 8, 15]), ALU.mult), m, zc, res["sc"])
                    cbk[par_].free = [c1]
                for a in range(2):
                    pa = p3[:, a * 8:a * 8 + 8, :]
                    mk = C("cmneg")[:, a * 16:a * 16 + 15].rearrange("p (o n) -> p o n", o=1).to_broadcast([P, 8, 15])
                    c2 = dve(lambda e, pa=pa, mk=mk: e.tensor_tensor(pa, pa, mk, ALU.add), c1)
                c3 = dve(lambda e: e.tensor_reduce(mx16, p3, AX, ALU.max), c2)
                c4 = dve(lambda e: e.tensor_tensor(p3, p3, bc(mx16), ALU.subtract), c3)
                c5 = act(lambda e: e.activation(p3, p3, ACT.Exp), c4)
                yield
                c6 = dve(lambda e: e.tensor_reduce(mx16, p3, AX, ALU.add), c5)
                c7 = dve(lambda e: e.reciprocal(w16, mx16), c6)
                g0 = gt.rearrange("p (r j) -> p r j", j=3)[:, :, 0]
                c8 = dve(lambda e: e.tensor_tensor(w16, w16, g0, ALU.mult), c7, gfin)
                for a in range(2):
                    pa = p3[:, a * 8:a * 8 + 8, :]
                    mk = C("cm01")[:, a * 16:a * 16 + 15].rearrange("p (o n) -> p o n", o=1).to_broadcast([P, 8, 15])
                    c9 = dve(lambda e, pa=pa, mk=mk: e.tensor_tensor(pa, pa, mk, ALU.mult), c6)
                c10 = dve(lambda e: e.tensor_tensor(p3, p3, bc(w16), ALU.mult), c8, c9)
                yield
                bank = side[2]
                for a in range(2):
                    tr = pe(lambda e, a=a, bank=bank: e.transpose(bank.t[:, a * P:a * P + P], Pc[:, a * P:a * P + P], ident), c10, bank.free)
                e4 = act(lambda e, bank=bank: e.activation(PcT, bank.t[:, 0:S], ACT.Copy), tr)
                bank.free = [e4]
                res["Pc"] = [e3, e4]
                yield

            def pre_for(pair):
                def pre(o, b):
                    pe(lambda e: e.matmul(o, Vb[:, pair * P:pair * P + P], PcT, start=True, stop=False, skip_group_check=True), res["Pc"], b.free)
                return pre

            def jobs():
                out_ = []
                for c in range(4):
                    for i, (hp, kind) in enumerate(((0, 0), (1, 0), (0, 1), (1, 1))):
                        h, o, g = 2 * c + hp, 64 * hp, c // 2
                        kb = (kind * 2 + g) * S
                        out_.append(dict(
                            q=lambda a, b_, c=c, o=o: qT[o:o + 64, c * S + a:c * S + b_],
                            k=lambda a, b_, kb=kb, o=o: kT[o:o + 64, kb + a:kb + b_],
                            sc=scq.rearrange("p (a h) -> p h a", a=2)[:, h, :], nsc=nscq.rearrange("p (a h) -> p h a", a=2)[:, h, :],
                            v=lambda s, kind=kind, g=g, hp=hp: vp[:, ((kind * 2 + s) * 2 + g) * 192 + 64 * (1 - hp):((kind * 2 + s) * 2 + g) * 192 + 64 * (1 - hp) + P],
                            gate=gt.rearrange("p (a r) -> p r a", a=2)[:, h * 3 + 1 + kind, :],
                            pair=c, first=i == 0, last=i == 3, pre=pre_for(c)))
                return out_

            def y_out(pair, b, m):
                lo = split_y(4 + pair, b.t[:, 0:S], m, Y["readers"])
                b.free = [lo]
                res["y"].append(lo)

            def attn():
                yield from compressed()
                yield from softmax_heads(jobs(), [res["kT", 0], res["kT", 1], res["qT", 0], res["qT", 1], res["sc"], gfin], scq, nscq, vops, y_out)

            while bg:
                tick()
            res["kdone"] = [res["qT", 1]]
            b, fin = tok_group("Mmv", 512, step)
            mvo = []
            for a in range(2):
                dst = mv[:, a * 520:a * 520 + 520].rearrange("p (h y) -> p h y", y=130)[:, :, 0:P]
                mvo.append(act(lambda e, a=a, b=b, dst=dst: e.activation(dst, b[a].t[:, :].rearrange("p (h y) -> p h y", y=P), ACT.Copy), fin[a], z3))
                b[a].free = [mvo[-1]]
            b, fin = tok_group("Mmo", 512, step)
            gm = []
            for a in range(2):
                g = gmo[:, a * 512:a * 512 + 512]
                t1 = act(lambda e, a=a, b=b, g=g: e.activation(g, b[a].t[:, :], ACT.Tanh, scale=0.5), fin[a], start)
                b[a].free = [t1]
                gm.append(dve(lambda e, g=g: e.scalar_tensor_tensor(g, g, 1.0, PR("on"), ALU.add, ALU.mult), t1))

            mb = [banks[2], banks[3]]
            gate_ring = Ring([banks[0], banks[1]])

            def mlstm():
                mrow = rows[1]
                for h in range(4):
                    c, o = h // 2, 64 * (h % 2)
                    E, PT = Eb[h % 2], Pb[h % 2]
                    bm, bs = mb
                    sel = C("sel")[0:4, h * P:h * P + P]
                    pe(lambda e, sel=sel: e.matmul(bm.t[:, 0:S], sel, mrow[0:4, 0:S], start=True, stop=False, skip_group_check=True), res["M"], bm.free)
                    pe(lambda e, sel=sel: e.matmul(bm.t[:, S:S + P], sel, mrow[0:4, P:S], start=False, stop=False, skip_group_check=True))
                    pe(lambda e: e.matmul(bm.t[:, 0:P], ident, C("bigT"), start=False, stop=False, skip_group_check=True))
                    m1 = pe(lambda e: e.matmul(bm.t[:, S:S + P], ident, C("bigT"), start=False, stop=True, skip_group_check=True))
                    e0 = act(lambda e, h=h, E=E: e.activation(E[:, 0:S], bm.t[:, 0:S], ACT.Exp, scale=-1.0, bias=acol[:, h:h + 1]), m1, res["cols"], convs, res.get(("mv", h % 2), []))
                    e1 = act(lambda e, h=h, E=E: e.activation(E[:, S:S + P], bm.t[:, S:S + P], ACT.Exp, scale=-1.0, bias=acol[:, 4 + h:5 + h]))
                    bm.free = [e1]
                    kk, qq = qkT[o:o + 64, (2 + c) * S:(3 + c) * S], qkT[o:o + 64, c * S:(c + 1) * S]
                    pe(lambda e, kk=kk, qq=qq: e.matmul(bs.t[:, 0:S], kk[:, 0:P], qq, start=True, stop=True, skip_group_check=True), convs, bs.free)
                    m2 = pe(lambda e, kk=kk, qq=qq: e.matmul(bs.t[:, S:S + P], kk[:, P:S], qq[:, P:S], start=True, stop=True, skip_group_check=True))
                    yield
                    p1 = dve(lambda e, E=E, PT=PT: e.scalar_tensor_tensor(PT, bs.t[:, 0:S + P], 1.0 / 32, E, ALU.mult, ALU.mult), m2, e0, e1, res.get(("mv", h % 2), []))
                    bs.free = [p1]
                    res["mv", h % 2] = [p1]
                    yield
                    ve = lambda a, h=h: mv[:, a * 520 + h * 130:a * 520 + h * 130 + 130]
                    pe(lambda e, PT=PT, ve=ve: e.matmul(bm.t[:, 0:130], PT[:, 0:P], ve(0), start=True, stop=True), p1, mvo, bm.free)
                    pe(lambda e, PT=PT, ve=ve: e.matmul(bm.t[:, 130:260], PT[:, P:S], ve(0), start=True, stop=False))
                    m3 = pe(lambda e, PT=PT, ve=ve: e.matmul(bm.t[:, 130:260], PT[:, S:S + P], ve(1), start=False, stop=True))
                    res["mv", h % 2] = [p1, m3]
                    den = bm.t[:, 0:260].rearrange("p (a y) -> p a y", a=2)[:, :, P]
                    ec = ecol.rearrange("p (a h) -> p h a", a=2)[:, h, :]
                    d2 = dcol[:, 4 * h:4 * h + 2]
                    d0 = dve(lambda e, den=den, ec=ec, d2=d2: e.scalar_tensor_tensor(d2, den, -1.0, ec, ALU.mult, ALU.max), m3, res["cols"])
                    d1 = dve(lambda e, den=den, d2=d2: e.tensor_tensor(d2, den, d2, ALU.max), d0)
                    dr = dve(lambda e, d2=d2: e.reciprocal(d2, d2), d1)
                    for a in range(2):
                        ha = hm[:, a * 512 + h * P:a * 512 + h * P + P]
                        n1 = dve(lambda e, a=a, ha=ha, d2=d2: e.tensor_scalar(ha, bm.t[:, a * 130:a * 130 + P], d2[:, a:a + 1], None, ALU.mult), dr, res["X"], res["cmp"])
                        s1 = act(lambda e, a=a, h=h, ha=ha, E=E: e.activation(E[:, a * P:a * P + P], ha, ACT.Square, accum_out=ms[:, a * 4 + h:a * 4 + h + 1]), n1, p1)
                    bm.free = [n1]
                    res["mv", h % 2] = [p1, m3, s1]
                    yield
                k1 = pool(lambda e: e.tensor_scalar(ms, ms, 4.0 / 128, None, ALU.mult), s1)
                rs = rsqrt(ms, ms, 4 * EPS, k1)
                for a in range(2):
                    for h in range(4):
                        ha = hm[:, a * 512 + h * P:a * 512 + h * P + P]
                        n2 = dve(lambda e, a=a, h=h, ha=ha: e.scalar_tensor_tensor(ha, ha, ms[:, a * 4 + h:a * 4 + h + 1], gmo[:, a * 512 + h * P:a * 512 + h * P + P], ALU.mult, ALU.mult), rs, gm)
                    bank = mb[a]
                    for h in range(4):
                        tr = pe(lambda e, a=a, h=h, bank=bank: e.transpose(bank.t[:, h * P:h * P + P], hm[:, a * 512 + h * P:a * 512 + h * P + P], ident), n2, bank.free)
                    dst = lambda buf, a=a: buf[:, 0:4 * S].rearrange("p (k t) -> p k t", t=S)[:, :, a * P:a * P + P]
                    src = bank.t[:, :].rearrange("p (k t) -> p k t", t=P)
                    hi = act(lambda e, dst=dst, src=src: e.activation(dst(yhi), src, ACT.Copy), tr, Y["readers"])
                    lo = dve(lambda e, dst=dst, src=src: e.tensor_tensor(dst(ylo), src, dst(yhi).bitcast(F32), ALU.subtract), hi)
                    bank.free = [lo]
                    res["y"].append(lo)
                    yield

            bg.append(attn())
            bg2.append(mlstm())
            work.items, keep = gate_ring.items, work.items
            gates_free[0] = [res["cmp"], res["qT", 0], res["qT", 1]]
            for f in range(KD):
                for gmm in gate_block("M", f, hb16):
                    tick(3)
            while bg or bg2:
                tick()
            work.items = keep
            H["readers"] = [gmm]
            mm, xr = merge_tail("M", res["y"])
            arena_free[0] = [mm, res["y"][-1]]
            return xr

        fw, fb = PR("fw"), PR("fbias")
        pads = Ring([Bank(arena[:, 2048:2048 + 258]), Bank(arena[:, 2320:2320 + 258])])
        cvb = Ring([Bank(arena[:, 2600:2600 + S]), Bank(arena[:, 2860:2860 + S])])

        def conv_hidden(i, b, up):
            s, p, ap, cv = sil_ring.get(), prod_ring.get(), pads.get(), cvb.get()
            a1 = act(lambda e: e.activation(ap.t[:, 2:258], b.t[:, 0:S], ACT.Copy), up, ap.free)
            c1 = dve(lambda e: e.tensor_scalar(cv.t, ap.t[:, 2:258], fw[:, 3 * i + 2:3 * i + 3], fb[:, i:i + 1], ALU.mult, ALU.add), a1, cv.free)
            c2 = dve(lambda e: e.scalar_tensor_tensor(cv.t, ap.t[:, 1:257], fw[:, 3 * i + 1:3 * i + 2], cv.t, ALU.mult, ALU.add), c1)
            c3 = dve(lambda e: e.scalar_tensor_tensor(cv.t, ap.t[:, 0:S], fw[:, 3 * i:3 * i + 1], cv.t, ALU.mult, ALU.add), c2)
            ap.free = [c3]
            g1 = act(lambda e: e.activation(s.t[:, :], cv.t, ACT.Gelu), c3, s.free)
            cv.free = [g1]
            m1 = dve(lambda e: e.tensor_tensor(p.t[:, :], s.t[:, :], b.t[:, S:2 * S], ALU.mult), g1, p.free)
            b.free, s.free = [m1], [m1]
            hb, lo = split_hidden(p.t[:, :], m1)
            p.free = [lo]
            return hb, lo

        xr = [[ld_x], [ld_x]]
        par_dram_pw = [gains[8 + l][:, 0:512] for l in range(2)]
        for l in range(2):
            norm(xr)
            xr = ffn(f"L{l}f1", swiglu_hidden, 0.5)
            if stop == f"L{l}f1":
                break
            norm(xr)
            load_pool_w(l)
            xr = mixer1(l)
            if stop == f"L{l}m":
                break
            norm(xr)
            xr = ffn(f"L{l}f2", swiglu_hidden, 0.5)
            if stop == f"L{l}f2":
                break
        if stop is None or stop[0] == "M":
            norm(xr)
            xr = mixer2()
        if stop is None:
            norm(xr)
            zp = [pool(lambda e, q=q: e.memset(q.t, 0.0), arena_free[0]) for q in pads.items]
            for q in pads.items:
                q.free = zp
            cvb.items[0].free = cvb.items[1].free = list(arena_free[0])
            xr = ffn("Mf", conv_hidden, 1.0)
        st_out = Q.dma("st_out", lambda e: e.dma_start(out.rearrange("(a p) n -> p a n", p=P), x[:, :].rearrange("p (a n) -> p a n", a=2)), xr[0], xr[1])
        fin = Q.put("sp", lambda e: e.nop(), st_out)
        Q.number()
        names = sorted({op.sem for q in Q.q.values() for op in q if op.signals})
        sems = {s: ctx.enter_context(nc.semaphore(f"s_{s}")) for s in names}
        block = ctx.enter_context(nc.Block())

        @block.sync
        def _(e):
            Q.run("sp", e, sems)

        @block.scalar
        def _(e):
            Q.run("act", e, sems)

        @block.vector
        def _(e):
            Q.run("dve", e, sems)

        @block.tensor
        def _(e):
            Q.run("pe", e, sems)

        @block.gpsimd
        def _(e):
            Q.run("pool", e, sems)



def kmajor(w, k0=0, nk=KD):
    return w[k0 * P:(k0 + nk) * P].reshape(nk, P, -1).transpose(1, 0, 2).reshape(P, -1)


def pack_weights(I, plan):
    g = lambda n: np.asarray(I[n])
    src = {}

    def ffn(tag, wu, wd):
        for i in range(NF):
            src[f"{tag}a{i}"] = lambda i=i: kmajor(wu[:, i * P:(i + 1) * P])
            src[f"{tag}b{i}"] = lambda i=i: kmajor(wu[:, DFF + i * P:DFF + (i + 1) * P])
            src[f"{tag}d{i}"] = lambda i=i: wd[i * P:(i + 1) * P]

    def tail(tag, w0, w1, wo):
        for i in range(KD):
            src[f"{tag}br{i}"] = lambda i=i: np.concatenate([kmajor(w0[:, i * P:(i + 1) * P], 0, 4), kmajor(w1[:, i * P:(i + 1) * P], 0, 4)], 1)
            src[f"{tag}wo{i}"] = lambda i=i: wo[i * P:(i + 1) * P]

    def group(tag, w):
        for k, m in a_group(w.shape[1]):
            src[f"{tag}{k}"] = lambda k=k, m=m: kmajor(w, k, m)

    for l in range(2):
        ffn(f"L{l}f1", g("ffn1_w_gate_up")[l], g("ffn1_w_down")[l])
        ffn(f"L{l}f2", g("ffn2_w_gate_up")[l], g("ffn2_w_down")[l])
        wi = g("w_in")[l]
        for j, nm in enumerate("uqkv"):
            group(f"L{l}{nm}", wi[:, j * 512:(j + 1) * 512])
        for f in range(KD):
            for j in range(2):
                src[f"L{l}g{j}{f}"] = lambda wi=wi, f=f, j=j: kmajor(wi[:, 2048 + j * D + f * P:2048 + j * D + (f + 1) * P])
        tail(f"L{l}", g("w_branch_pool")[l], g("w_branch_attn")[l], g("w_out")[l])
    w2 = g("w_in_2")[0]
    col = lambda a, n: w2[:, a:a + n]
    group("Mk3", np.concatenate([col(2056, 128), col(2312, 128), col(2568, 128), col(2184, 128)], 1))
    group("Mv3", np.concatenate([col(2440, 128), col(2696, 128), col(1536, 8), col(2824, 24)], 1))
    group("Mnq", col(1544, 512))
    group("Mmv", col(512, 512))
    group("Mmo", col(1024, 512))
    for f in range(4):
        src[f"Mqk{f}"] = lambda f=f: kmajor(w2[:, f * P:(f + 1) * P])
    for f in range(KD):
        for j in range(2):
            src[f"Mg{j}{f}"] = lambda f=f, j=j: kmajor(w2[:, 2848 + j * D + f * P:2848 + j * D + (f + 1) * P])
    for nm in "kv":
        w1 = g(f"cmp_{nm}_w1_2")[0]
        for i in range(4):
            src[f"M{nm}w1{i}"] = lambda w1=w1, i=i: kmajor(w1, 4 * i, 4)
    tail("M", g("w_up_m_2")[0], g("w_up_n_2")[0], g("w_out_2")[0])
    ffn("Mf", g("ffn_w_up_2")[0], g("ffn_w_down_2")[0])
    total = plan[-1][3] + plan[-1][1]
    out = np.empty(total * P, np.float32)
    for name, n, _, off in plan:
        out[off * P:(off + n) * P] = src[name]().reshape(-1)
    return out


def pack_params(I, pat, n):
    g = lambda k: np.asarray(I[k])
    out = np.zeros((P, n), np.float32)

    def put(name, a):
        out[:a.shape[0], pat[name][0]:pat[name][1]] = a

    cols = lambda v: v.reshape(-1, P).T
    rows = lambda v: np.broadcast_to(v.reshape(1, -1), (P, v.size))
    for l in range(2):
        put(f"bg{l}", cols(g("b_gate")[l]))
        put(f"ps{l}", cols(g("pool_scale")[l]))
        put(f"qn{l}", rows(g("q_norm")[l]))
        put(f"kn{l}", rows(g("k_norm")[l]))
    put("mg", cols(g("merge_gate_b_2")[0]))
    put("cw", g("m_conv_w_2")[0].reshape(4, 4, P).transpose(2, 1, 0).reshape(P, 16))
    put("cb", cols(g("m_conv_b_2")[0]))
    put("ib", g("m_igate_b_2")[0].reshape(4, 1))
    put("fb", g("m_fgate_b_2")[0].reshape(4, 1))
    put("on", rows(g("m_out_norm_w_2")[0]))
    put("qn2", rows(g("q_norm_w_2")[0]))
    put("kn3", np.concatenate([rows(g(k)[0]) for k in ("kcmp_norm_w_2", "kslc_norm_w_2", "kwin_norm_w_2")], 1))
    put("kpe", g("cmp_k_pe_2")[0].reshape(16, P).T)
    put("vpe", g("cmp_v_pe_2")[0].reshape(16, P).T)
    put("fw", g("ffn_conv_w_2")[0].reshape(3, NF, P).transpose(2, 1, 0).reshape(P, -1))
    put("fbias", cols(g("ffn_conv_b_2")[0]))
    kw2, vw2 = g("cmp_k_w2_2")[0], g("cmp_v_w2_2")[0]
    put("kw2", np.concatenate([kw2[0:P], kw2[0:P], kw2[P:], kw2[P:]], 1))
    put("vw2", np.concatenate([vw2[0:P], vw2[0:P], vw2[P:], vw2[P:]], 1))
    return out


def pack_gains(I):
    g = lambda k: np.asarray(I[k])
    rows = [g("ffn1_norm")[0], g("mix_norm")[0], g("ffn2_norm")[0], g("ffn1_norm")[1], g("mix_norm")[1], g("ffn2_norm")[1],
            g("norm1_w_2")[0], g("norm2_w_2")[0]]
    out = np.zeros((10, P, D), np.float32)
    for i, r in enumerate(rows):
        out[i] = r.reshape(1, -1)
    for l in range(2):
        out[8 + l, :, 0:512] = g("pool_w")[l].transpose(1, 0, 2).reshape(P, 512)
    return out


STOP = None


def kernel(**inputs):
    import concourse.bacc as _bacc
    from concourse.bass_utils import run_bass_kernel_spmd as _run

    nc = _bacc.Bacc("TRN2", target_bir_lowering=False, num_devices=1)
    const, cat = constants()
    pat, npar = params_layout()
    plan, _ = tile_plan()
    arrays = {
        "x_dram": np.ascontiguousarray(np.asarray(inputs["x"]).reshape(S, D)),
        "w_dram": pack_weights(inputs, plan),
        "g_dram": pack_gains(inputs),
        "c_dram": const,
        "p_dram": pack_params(inputs, pat, npar),
    }
    aps = {n: nc.dram_tensor(n, a.shape, mybir.dt.float32, kind="ExternalInput").ap() for n, a in arrays.items()}
    out = nc.dram_tensor("out_dram", (S, D), mybir.dt.float32, kind="ExternalOutput").ap()
    build_program(nc, aps["x_dram"], aps["w_dram"], aps["g_dram"], aps["c_dram"], aps["p_dram"], out, cat, pat, plan, STOP)
    r = _run(nc, [arrays], core_ids=[0])
    return r.results[0]["out_dram"].reshape(1, S, D)
```

```python
import math
from contextlib import ExitStack

import numpy as np

import concourse.bass as bass
from concourse import mybir

ALU = mybir.AluOpType
ACT = mybir.ActivationFunctionType
F32 = mybir.dt.float32
F32R = mybir.dt.float32r
AX = mybir.AxisListType.X

P = 128
S = 256
D = 1024
KD = D // P
DFF = 2816
NF = DFF // P
EPS = 1e-6
TW = 1024
NRAW = 5
NSPL = 6
AHEAD = 5
LAST = 4
NEG = -1.0e30


def constants():
    c = {}
    c["ident"] = np.eye(P, dtype=np.float32)
    t = np.arange(P)
    tri = np.where(t[None, :] > t[:, None], np.float32(NEG), np.float32(0)).astype(np.float32)
    c["cmask"] = np.concatenate([tri, np.zeros((P, P), np.float32), tri], 1)
    c["bigT"] = np.where(t[:, None] > t[None, :], np.float32(1e30), np.float32(0)).astype(np.float32)
    half = 32
    inv = (np.float32(1.0) / (np.float32(10000.0) ** (np.arange(half, dtype=np.float32) * np.float32(2.0 / 64)))).astype(np.float32)
    ang = (np.arange(S, dtype=np.float32)[:, None] * inv[None, :]).astype(np.float32)
    cos, sin = np.cos(ang).astype(np.float32), np.sin(ang).astype(np.float32)
    cs = np.concatenate([cos, cos], 1).reshape(2, P, 64)
    sn = np.concatenate([-sin, sin], 1).reshape(2, P, 64)
    c["cos"] = cs.transpose(1, 0, 2).reshape(P, 128)
    c["sin"] = sn.transpose(1, 0, 2).reshape(P, 128)
    pm = []
    tt = np.arange(S)
    for w in (2, 4, 8, 16):
        lo = np.maximum(tt + 1 - w, 0)
        cnt = (tt + 1 - lo).astype(np.float32)
        s = np.arange(S)[:, None]
        m = np.where((s >= lo[None, :]) & (s <= tt[None, :]), np.float32(1) / cnt[None, :], np.float32(0))
        m = m - np.eye(S)
        pm += [m[0:P, :], m[P:S, P:S]]
    c["pool"] = np.concatenate(pm, 1).astype(np.float32)
    n = np.arange(15)
    cm = np.zeros((P, 2, 16), np.float32)
    for k in range(2):
        cm[:, k, :15] = (16 * n[None, :] + 31 <= (k * P + t)[:, None])
    c["cm01"] = cm.reshape(P, 32)
    c["cmneg"] = ((cm.astype(np.float64) - 1) * 1e30).astype(np.float32).reshape(P, 32)
    r = np.zeros((P, 2, 8, 16), np.float32)
    for h in range(8):
        for i in range(15):
            r[i, h // 4, h, i] = 1
    c["rep"] = r.reshape(P, 256)
    bd = np.zeros((8, 16, 4, 2, 64), np.float32)
    for h in range(8):
        bd[h, :, h // 2, h % 2, :] = 1
    c["bd"] = bd.reshape(P, 512)
    sel = np.zeros((P, 4, P), np.float32)
    for h in range(4):
        sel[h, h, :] = 1
    c["sel"] = sel.reshape(P, 512)
    names, at, off = [k for k in c if k != "pool"] + ["pool"], {}, 0
    for k in names:
        at[k] = (off, off + c[k].shape[1])
        off += c[k].shape[1]
    return np.ascontiguousarray(np.concatenate([c[k] for k in names], 1)), at


def params_layout():
    at, off = {}, 0
    for name, n in ([(f"bg{l}", 16) for l in range(2)] + [(f"ps{l}", 4) for l in range(2)]
                    + [(f"qn{l}", 64) for l in range(2)] + [(f"kn{l}", 64) for l in range(2)]
                    + [("mg", 16), ("cw", 16), ("cb", 4), ("ib", 1), ("fb", 1), ("on", 512), ("qn2", 64),
                       ("kn3", 192), ("kpe", 16), ("vpe", 16), ("fw", 3 * NF), ("fbias", NF),
                       ("kw2", 256), ("vw2", 256)]):
        at[name] = (off, off + n)
        off += n
    return at, off



def a_group(n):
    per = TW // n
    return [(k, min(per, KD - k)) for k in range(0, KD, per)]


L2_GROUPS = [("k3", 512), ("nq", 512), ("v3", 288), ("mv", 512), ("mo", 512)]


def tile_plan():
    plan = []

    def ffn(tag):
        plan.extend((f"{tag}p{k}", m * 512, True) for k, m in a_group(512))
        for i in range(2, NF):
            plan.extend([(f"{tag}a{i}", TW, True), (f"{tag}b{i}", TW, True)])
            if 3 <= i < NF - 1:
                plan.append((f"{tag}d{i - 3}", TW, True))
        plan.extend((f"{tag}d{i}", TW, True) for i in range(NF - LAST, NF))

    def tail(tag):
        for i in range(KD):
            plan.append((f"{tag}br{i}", TW, True))
            if 3 <= i < KD - 1:
                plan.append((f"{tag}wo{i - 3}", TW, True))
        plan.extend((f"{tag}wo{i}", TW, True) for i in range(KD - LAST, KD))

    for l in range(2):
        ffn(f"L{l}f1")
        for g in ("k", "q", "u", "v"):
            for k, m in a_group(512):
                plan.append((f"L{l}{g}{k}", m * 512, True))
        for f in range(KD):
            plan.extend([(f"L{l}g0{f}", TW, True), (f"L{l}g1{f}", TW, True)])
        tail(f"L{l}")
        ffn(f"L{l}f2")
    for g, n in L2_GROUPS[:3]:
        for k, m in a_group(n):
            plan.append((f"M{g}{k}", m * n, True))
    plan.append(("Mqk0", TW, True))
    for i in range(8):
        plan.append((f"M{'kv'[i // 4]}w1{i % 4}", TW, False))
    for f in range(1, 4):
        plan.append((f"Mqk{f}", TW, True))
    for g, n in L2_GROUPS[3:]:
        for k, m in a_group(n):
            plan.append((f"M{g}{k}", m * n, True))
    for f in range(2 * KD):
        plan.append((f"Mg{f % 2}{f // 2}", TW, True))
    tail("M")
    ffn("Mf")
    off, out = 0, []
    for name, n, split in plan:
        out.append((name, n, split, off))
        off += n
    return out, off


class Op:

    def __init__(self, eng, emit, waits, sem=None, value=0):
        self.eng, self.emit, self.waits, self.sem, self.value = eng, emit, waits, sem, value
        self.signals = sem is not None


class Queues:

    def __init__(self):
        self.q = {e: [] for e in ("pe", "act", "dve", "pool", "sp")}
        self.dma_count = {}

    def put(self, eng, emit, *waits):
        flat, todo = [], list(waits)
        while todo:
            w = todo.pop()
            if isinstance(w, (list, tuple)):
                todo.extend(w)
            else:
                w.signals = True
                flat.append(w)
        op = Op(eng, emit, flat)
        self.q[eng].append(op)
        return op

    def dma(self, sem, emit, *waits, eng="sp"):
        op = self.put(eng, emit, *waits)
        self.dma_count[sem] = self.dma_count.get(sem, 0) + 16
        op.sem, op.value, op.signals = sem, self.dma_count[sem], True
        return op

    def number(self):
        for eng, ops in self.q.items():
            n = 0
            for op in ops:
                if op.signals and op.sem is None:
                    n += 1
                    op.sem, op.value = eng, n

    def run(self, eng, handle, sems):
        seen = {}
        for op in self.q[eng]:
            need = {}
            for w in op.waits:
                need[w.sem] = max(need.get(w.sem, 0), w.value)
            for s, v in need.items():
                if seen.get(s, 0) < v:
                    handle.wait_ge(sems[s], v)
                    seen[s] = v
            ins = op.emit(handle)
            if op.signals:
                ins.then_inc(sems[op.sem], 16 if op.value and op.sem in self.dma_count else 1)


class Bank:
    def __init__(self, t):
        self.t, self.free = t, []


class Ring:

    def __init__(self, items):
        self.items, self.n = items, 0

    def get(self):
        b = self.items[self.n % len(self.items)]
        self.n += 1
        return b


def build_program(nc, x_in, wstream, gains, const_in, par_in, out, cat, pat, plan):
    Q = Queues()
    pe = lambda f, *w: Q.put("pe", f, *w)
    act = lambda f, *w: Q.put("act", f, *w)
    dve = lambda f, *w: Q.put("dve", f, *w)
    pool = lambda f, *w: Q.put("pool", f, *w)

    with ExitStack() as ctx:
        def sb(name, cols, dt=F32, parts=P):
            return ctx.enter_context(nc.sbuf_tensor(name, [parts, cols], dt))

        raw = sb("raw", NRAW * TW)
        whi = sb("whi", NSPL * TW, F32R)
        wlo = sb("wlo", NSPL * TW, F32R)
        x = sb("x", 2 * D)
        hhi = sb("hhi", KD * S, F32R)
        hlo = sb("hlo", KD * S, F32R)
        gain = sb("gain", D)
        cst = sb("cst", cat["pool"][0])
        par = sb("par", par_in.shape[1])
        hid = [sb(f"hid{i}", 2 * S, F32R) for i in range(4)]
        sil = [sb(f"sil{i}", S) for i in range(2)]
        prod = [sb(f"prod{i}", S) for i in range(2)]
        gates = sb("gates", KD * 2 * S)
        arena = sb("arena", 12832)
        yhi = sb("yhi", 8 * S, F32R)
        ylo = sb("ylo", 8 * S, F32R)
        small = sb("small", 560)
        banks = [Bank(ctx.enter_context(nc.psum_tensor(f"bank{i}", [P, 512], F32))) for i in range(8)]
        work = Ring(banks[0:4])
        side = banks[4:8]

        C = lambda name: cst[:, cat[name][0]:cat[name][1]]
        PR = lambda name: par[:, pat[name][0]:pat[name][1]]
        ident = C("ident")

        load_x = lambda a: Q.dma(f"ld_x{a}", lambda e: e.dma_start(x[:, a * D:a * D + D], x_in[a * P:a * P + P, :]))
        ld_x = [load_x(0)]
        gain_free = [[]]
        gain_no = [0]

        def load_gain():
            i = gain_no[0]
            gain_no[0] += 1
            return Q.dma("ld_gain", lambda e: e.dma_start(gain[:, :], gains[i]), *gain_free[0])

        ld_g = [load_gain()]
        ld_i = Q.dma("ld_i", lambda e: e.dma_start(ident, const_in[:, 0:P]))

        mhalf = small[:, 160:176]
        mh = pool(lambda e: e.memset(mhalf, -0.5))
        act(lambda e: e.activation(small[:, 12:13], mhalf[:, 0:1], ACT.Square), mh)

        def rsqrt(out_, in_, eps, *ready):
            n = out_.shape[1]
            o = pool(lambda e: e.tensor_scalar(out_, in_, eps, None, ALU.add), *ready)
            return pool(lambda e: e.tensor_tensor(out_, out_, mhalf[:, 0:n], ALU.pow), o, mh)

        class Tile:
            pass

        tiles = []
        raw_free = [[] for _ in range(NRAW)]
        spl_free = [None] * NSPL
        state = {"dma": 0, "split": 0, "next": 0}

        def issue_dma():
            j = state["dma"]
            if j >= len(plan):
                return
            name, n, split, off = plan[j]
            t = Tile()
            t.name, t.n, t.split, t.slot = name, n, split, j % NRAW
            t.raw = raw[:, t.slot * TW:t.slot * TW + n]
            t.load = Q.dma(f"raw{t.slot}", lambda e, t=t, off=off, n=n: e.dma_start(t.raw, wstream[off * P:(off + n) * P].rearrange("(p n) -> p n", p=P)),
                           *raw_free[t.slot])
            raw_free[t.slot] = None
            tiles.append(t)
            state["dma"] += 1

        def issue_split():
            j = state["split"]
            if j >= len(plan):
                return
            while state["dma"] <= j:
                issue_dma()
            t = tiles[j]
            state["split"] += 1
            if not t.split:
                finish_splits(j - 1)
                t.ready = [t.load]
                return
            s, n = j % NSPL, t.n
            assert spl_free[s] != "held"
            t.hi, t.lo = whi[:, s * TW:s * TW + n], wlo[:, s * TW:s * TW + n]
            prior = [spl_free[s]] if spl_free[s] is not None else []
            t.first = act(lambda e: e.activation(t.hi, t.raw, ACT.Copy), t.load, *prior)
            t.spl, spl_free[s] = s, "held"
            t.j = j
            late.append(t)
            finish_splits(j - 1)

        late = []

        def finish_splits(j, eng="dve"):
            while late and late[0].j <= j:
                t = late.pop(0)
                lo = Q.put(eng, lambda e, t=t: e.tensor_tensor(t.lo, t.raw, t.hi.bitcast(F32), ALU.subtract), t.first)
                raw_free[t.slot] = [lo]
                t.ready = [t.first, lo]
                issue_dma_upto(t.j + NRAW)

        def issue_dma_upto(j):
            while state["dma"] <= min(j, len(plan) - 1) and raw_free[state["dma"] % NRAW] is not None:
                issue_dma()

        def pump(upto):
            while state["split"] <= min(upto, len(plan) - 1):
                if plan[state["split"]][2] and spl_free[state["split"] % NSPL] == "held":
                    break
                if state["dma"] <= state["split"] and raw_free[state["split"] % NRAW] is None:
                    break
                issue_split()

        def next_tile(name, ahead=AHEAD):
            j = state["next"]
            state["next"] += 1
            pump(j + ahead)
            finish_splits(j)
            t = tiles[j]
            assert t.name == name, (t.name, name)
            return t

        def release(t, mm):
            if t.split:
                spl_free[t.spl] = mm
            else:
                raw_free[t.slot] = [mm]
                issue_dma_upto(state["next"] - 1 + NRAW)

        issue_dma_upto(0)
        issue_dma_upto(1)
        ld_x.append(load_x(1))
        issue_dma_upto(2)
        ld_c, ld_p = [], []

        def load_constants():
            ld_c.append(Q.dma("ld_c", lambda e: e.dma_start(cst[:, P:], const_in[:, P:cat["pool"][0]])))
            ld_p.append(Q.dma("ld_p", lambda e: e.dma_start(par[:, :], par_in)))

        issue_dma_upto(NRAW - 1)

        def mm3(psum, shi, slo, mhi, mlo, first, last, waits=()):
            pe(lambda e: e.matmul(psum, shi, mhi, start=first, stop=False, skip_group_check=True), *waits)
            pe(lambda e: e.matmul(psum, shi, mlo, start=False, stop=False, skip_group_check=True))
            return pe(lambda e: e.matmul(psum, slo, mhi, start=False, stop=last, skip_group_check=True))

        H = {"ready": [[], []], "readers": [], "second": None}

        def hT(buf, k, a=0, b=S):
            return buf[:, k * S + a:k * S + b]

        def feat_block(name, psum, first_waits, nk=KD, hi=hhi, lo=hlo, ready=None, part=0, t=None, tick=None, keep=False):
            t = t or next_tile(name)
            ready = [[H["ready"]]] + [[]] * (nk - 1) if ready is None else ready
            for k in range(nk):
                w = (part * nk + k) * P
                mm = mm3(psum, t.hi[:, w:w + P], t.lo[:, w:w + P], hT(hi, k), hT(lo, k),
                         k == 0, k == nk - 1, (t.ready, first_waits, ready[0]) if k == 0 else (ready[k],))
                if tick and k == nk // 2 - 1:
                    tick()
            if not keep:
                release(t, mm)
            if tick:
                tick()
            return mm

        def tok_group(tag, n, tick=None, first=False):
            b = [work.get(), work.get()]
            fin = [None, None]
            groups = a_group(n)

            def part(t, k0, m, a):
                for k in range(k0, k0 + m):
                    mv = (k - k0) * n
                    fin[a] = mm3(b[a].t[:, 0:n], hT(hhi, k, a * P, a * P + P), hT(hlo, k, a * P, a * P + P),
                                 t.hi[:, mv:mv + n], t.lo[:, mv:mv + n], k == 0, k == KD - 1,
                                 (t.ready, H["ready"][a][k // 4], b[a].free) if k == k0 or k == 4 else ())

            if first:
                ts = [next_tile(f"{tag}{k0}", 0) for k0, _ in groups]
                for a in range(2):
                    for t, (k0, m) in zip(ts, groups):
                        if a == 0 and t is ts[-1]:
                            H["second"]()
                            pump(state["next"] - 1 + AHEAD)
                        part(t, k0, m, a)
                        if a == 1:
                            release(t, fin[1])
                finish_splits(state["split"] - 1)
            else:
                for k0, m in groups:
                    t = next_tile(f"{tag}{k0}")
                    for a in range(2):
                        part(t, k0, m, a)
                        if a == 1:
                            release(t, fin[1])
                        if tick:
                            tick()
            H["readers"] = [fin[1]]
            return b, fin

        def accum_half(t, a, shi, slo, ready, first, last):
            for h in range(2):
                mm = mm3(side[2 * a + h].t[:, :], shi[:, a * P:a * P + P], slo[:, a * P:a * P + P],
                         t.hi[:, h * 512:h * 512 + 512], t.lo[:, h * 512:h * 512 + 512], first, last,
                         (t.ready, ready, side[2 * a + h].free) if h == 0 or first else ())
                if last:
                    acc_done[2 * a + h] = mm
            return mm

        def accum_block(name, hb, ready, first):
            t = next_tile(name)
            for a in range(2):
                mm = accum_half(t, a, hb.t[:, 0:S], hb.t[:, S:2 * S], ready, first, False)
            release(t, mm)
            hb.free = [mm]

        acc_done = [None] * 4
        st = small[:, 0:12]
        sqj = arena[:, 0:2048]
        xnb = arena[:, 2048:4096]
        tokbuf = arena[:, 5200:6224]
        arena_free = [[]]

        def stage_x(a, h, scale, ready=None):
            o = x[:, a * D + h * 512:a * D + h * 512 + 512]
            if ready is None:
                b = side[2 * a + h]
                ready = dve(lambda e: e.scalar_tensor_tensor(o, b.t[:, :], scale, o, ALU.mult, ALU.add), acc_done[2 * a + h])
                b.free = [ready]
            j = sqj[:, (2 * a + h) * 512:(2 * a + h) * 512 + 512]
            return act(lambda e: e.activation(j, o, ACT.Square, scale=1.0 / 32, accum_out=st[:, 4 * a + h:4 * a + h + 1]), ready, arena_free[0], mh)

        def stage_n(a, sq):
            c0 = st[:, 4 * a + 2:4 * a + 3]
            e1 = pool(lambda e: e.tensor_scalar(c0, st[:, 4 * a:4 * a + 1], st[:, 4 * a + 1:4 * a + 2], EPS, ALU.add, ALU.add), sq)
            rs = pool(lambda e: e.tensor_tensor(c0, c0, mhalf[:, 0:1], ALU.pow), e1)
            out_ = []
            for h in range(2):
                o = x[:, a * D + h * 512:a * D + h * 512 + 512]
                w = xnb[:, a * D + h * 512:a * D + h * 512 + 512]
                out_.append(dve(lambda e, o=o, w=w, h=h: e.scalar_tensor_tensor(w, o, c0, gain[:, h * 512:h * 512 + 512], ALU.mult, ALU.mult), rs, ld_g[0], arena_free[0]))
            return out_

        def stage_t(a, xn):
            fin = []
            for g in range(2):
                b = work.get()
                for k in range(4):
                    kk = 4 * g + k
                    tr = pe(lambda e, b=b, k=k, kk=kk: e.transpose(b.t[:, k * P:k * P + P], xnb[:, a * D + kk * P:a * D + kk * P + P], ident),
                            xn[g], b.free, ld_i)
                dst = lambda buf, g=g: buf[:, :].rearrange("p (k t) -> p k t", t=S)[:, 4 * g:4 * g + 4, a * P:a * P + P]
                src = b.t[:, :].rearrange("p (k t) -> p k t", t=P)
                hi = act(lambda e, dst=dst, src=src: e.activation(dst(hhi), src, ACT.Copy), tr, H["readers"])
                lo = dve(lambda e, dst=dst, src=src: e.tensor_tensor(dst(hlo), src, dst(hhi).bitcast(F32), ALU.subtract), hi)
                b.free = [lo]
                fin.append(lo)
            H["ready"][a] = fin
            return tr

        def second_half(xn1):
            def go():
                tr = stage_t(1, xn1)
                arena_free[0] = [tr]
            H["second"] = go
            gain_free[0] = [xn1[1]]
            if gain_no[0] < 8:
                ld_g[0] = load_gain()

        stores = []

        def finish_accum(items, scale, final=False):
            ts = [next_tile(n, 0) for n, _, _ in items]
            sq = [[], []]
            if final:
                pump(state["split"])

            def split_one(eng="dve"):
                pump(state["split"])
                finish_splits(state["split"] - 1, eng)

            def quarter(a, h, part):
                for i in part:
                    _, hb, ready = items[i]
                    t = ts[i]
                    mm = mm3(side[2 * a + h].t[:, :], hb.t[:, a * P:a * P + P], hb.t[:, S + a * P:S + a * P + P],
                             t.hi[:, h * 512:h * 512 + 512], t.lo[:, h * 512:h * 512 + 512], False, i == len(items) - 1, (t.ready, ready))
                    if a == h == 1:
                        release(t, mm)
                        hb.free = [mm]
                acc_done[2 * a + h] = mm

            every = range(len(items))
            if not final:
                split_one()
                pump(state["split"])
            quarter(0, 0, every[:-1])
            quarter(0, 1, every[:-1])
            quarter(0, 0, every[-1:])
            if final:
                final_quarter(0, 0, scale)
                quarter(0, 1, every[-1:])
                final_quarter(0, 1, scale)
                for h in range(2):
                    quarter(1, h, every)
                    final_quarter(1, h, scale)
                return
            sq[0].append(stage_x(0, 0, scale))
            quarter(0, 1, every[-1:])
            sq[0].append(stage_x(0, 1, scale))
            finish_splits(state["split"] - 1)
            xn0 = stage_n(0, sq[0])
            quarter(1, 0, every)
            sq[1].append(stage_x(1, 0, scale))
            quarter(1, 1, every[:1])
            stage_t(0, xn0)
            split_one("pool")
            quarter(1, 1, every[1:])
            pump(state["split"])
            sq[1].append(stage_x(1, 1, scale))
            finish_splits(state["split"] - 1)
            xn1 = stage_n(1, sq[1])
            second_half(xn1)

        def final_quarter(a, h, scale):
            o = x[:, a * D + h * 512:a * D + h * 512 + 512]
            b = side[2 * a + h]
            op = dve(lambda e: e.scalar_tensor_tensor(o, b.t[:, :], scale, o, ALU.mult, ALU.add), acc_done[2 * a + h])
            stores.append(Q.dma(f"st_out{a}{h}", lambda e: e.dma_start(out[a * P:a * P + P, h * 512:h * 512 + 512], o), op))

        hid_ring = Ring([Bank(h) for h in hid])
        sil_ring = Ring([Bank(h) for h in sil])
        prod_ring = Ring([Bank(h) for h in prod])

        def split_hidden(src, src_ready, extra=()):
            hb = hid_ring.get()
            hi = act(lambda e: e.activation(hb.t[:, 0:S], src, ACT.Copy), src_ready, hb.free)
            lo = dve(lambda e: e.tensor_tensor(hb.t[:, S:2 * S], src, hb.t[:, 0:S].bitcast(F32), ALU.subtract), hi)
            return hb, lo

        def v3d(ap, b, c):
            return ap.rearrange("p (b c) -> p b c", b=b, c=c)

        def ffn(tag, hidden_fn, scale, final=False, pointwise=True):
            pend = {}
            bt, fin = tok_group(f"{tag}p", 512, first=True)
            ev = []
            halves = lambda t: t.rearrange("p (n j f) -> p n j f", j=2, f=P)
            for a in range(2):
                tb = tokbuf[:, a * 512:a * 512 + 512]
                if not pointwise:
                    ev.append(act(lambda e, a=a, tb=tb: e.activation(tb, bt[a].t[:, :], ACT.Copy), fin[a], arena_free[0]))
                else:
                    s3, p3, bh = v3d(tb[:, 0:S], 2, P), v3d(tb[:, S:2 * S], 2, P), halves(bt[a].t[:, :])
                    s1 = act(lambda e, s3=s3, bh=bh: e.activation(s3, bh[:, :, 0, :], ACT.Silu), fin[a], arena_free[0])
                    ev.append(dve(lambda e, s3=s3, p3=p3, bh=bh: e.tensor_tensor(p3, s3, bh[:, :, 1, :], ALU.mult), s1, arena_free[0]))
                bt[a].free = [ev[a]]

            def from_tokens(n):
                bb = work.get()
                for j in range(2):
                    for a in range(2):
                        tr = pe(lambda e, j=j, a=a: e.transpose(bb.t[:, j * S + a * P:j * S + a * P + P],
                                tokbuf[:, a * 512 + (2 * n + j) * P:a * 512 + (2 * n + j + 1) * P], ident), ev[a], bb.free)
                return hidden_fn(n, bb, tr)

            def both_from_tokens():
                bb = work.get()
                for n in range(2):
                    for a in range(2):
                        tr = pe(lambda e, n=n, a=a: e.transpose(bb.t[:, n * S + a * P:n * S + a * P + P],
                                tokbuf[:, a * 512 + S + n * P:a * 512 + S + (n + 1) * P], ident), ev[a], bb.free)
                last = []
                for n in range(2):
                    pend[n] = split_hidden(bb.t[:, n * S:n * S + S], [tr, last])
                    last = pend[n][1]
                bb.free = [last]

            for i in range(2, NF):
                b = work.get()
                feat_block(f"{tag}a{i}", b.t[:, 0:S], b.free)
                if i == 2:
                    if not pointwise:
                        pend[0] = from_tokens(0)
                    else:
                        both_from_tokens()
                mm = feat_block(f"{tag}b{i}", b.t[:, S:2 * S], ())
                if i == 2 and not pointwise:
                    pend[1] = from_tokens(1)
                if i == NF - 1:
                    finish_splits(state["split"] - 1)
                pend[i] = hidden_fn(i, b, mm)
                if i == 5 and not ld_c:
                    load_constants()
                if 3 <= i < NF - 1:
                    accum_block(f"{tag}d{i - 3}", *pend.pop(i - 3), i == 3)
            H["readers"] = [mm]
            finish_accum([(f"{tag}d{i}", *pend.pop(i)) for i in range(NF - LAST, NF)], scale, final)

        def swiglu_hidden(i, b, up):
            s, p = sil_ring.get(), prod_ring.get()
            a1 = act(lambda e: e.activation(s.t[:, :], b.t[:, 0:S], ACT.Silu), up, s.free)
            m1 = dve(lambda e: e.tensor_tensor(p.t[:, :], s.t[:, :], b.t[:, S:2 * S], ALU.mult), a1, p.free)
            b.free, s.free = [m1], [m1]
            hb, lo = split_hidden(p.t[:, :], m1)
            p.free = [lo]
            return hb, lo

        def gate_block(tag, f, bias, tick):
            b = work.get()
            for j in range(2):
                mm = feat_block(f"{tag}g{j}{f}", b.t[:, j * S:j * S + S], b.free if j == 0 else (), tick=tick)
            ops = []
            for j in range(2):
                g = gates[:, (2 * f + j) * S:(2 * f + j + 1) * S]
                ops.append(act(lambda e, g=g, j=j: e.activation(g, b.t[:, j * S:j * S + S], ACT.Tanh, scale=0.5,
                                                                bias=bias[:, j * KD + f:j * KD + f + 1]), mm, halfb[0], gates_free[0]))
            b.free = ops
            gate_ops[f] = ops
            return mm

        gate_ops = {}
        halfb = [None]

        def merge_tail(tag, y_ready):
            pend = {}
            for i in range(KD):
                b = work.get()
                t = next_tile(f"{tag}br{i}")
                feat_block(None, b.t[:, 0:S], b.free, nk=4, hi=yhi, lo=ylo, ready=y_ready[0], part=0, t=t, keep=True)
                mm = feat_block(None, b.t[:, S:2 * S], (), nk=4, hi=yhi[:, 4 * S:8 * S], lo=ylo[:, 4 * S:8 * S],
                                ready=y_ready[1], part=1, t=t)
                if i == KD - 1:
                    finish_splits(state["split"] - 1)
                s, p = sil_ring.get(), prod_ring.get()
                g = [gates[:, (2 * i + j) * S:(2 * i + j + 1) * S] for j in range(2)]
                m0 = dve(lambda e, s=s, g=g, b=b: e.scalar_tensor_tensor(s.t[:, :], g[0], 1.0, b.t[:, 0:S], ALU.add, ALU.mult),
                         mm, gate_ops[i], s.free)
                m1 = dve(lambda e, p=p, g=g, b=b: e.scalar_tensor_tensor(p.t[:, :], g[1], 1.0, b.t[:, S:2 * S], ALU.add, ALU.mult),
                         p.free)
                m2 = dve(lambda e, s=s, p=p: e.tensor_tensor(p.t[:, :], s.t[:, :], p.t[:, :], ALU.add), m0, m1)
                b.free, s.free = [m1], [m2]
                hb, lo = split_hidden(p.t[:, :], m2)
                p.free = [lo]
                pend[i] = (hb, lo)
                if 3 <= i < KD - 1:
                    accum_block(f"{tag}wo{i - 3}", *pend.pop(i - 3), i == 3)
            Y["readers"] = [mm]
            arena_free[0] = [mm]
            finish_accum([(f"{tag}wo{i}", *pend.pop(i)) for i in range(KD - LAST, KD)], 0.5)

        A = {}

        def region(name, off, n):
            A[name] = arena[:, off:off + n]
            return A[name]

        def rope_tables(dst, w, nk, waits):
            ops = []
            for a in range(2):
                for k in range(nk):
                    wk = w[:, k * 64:k * 64 + 64]
                    c = dst[:, (a * nk + k) * 64:(a * nk + k + 1) * 64]
                    s = dst[:, ((2 + a) * nk + k) * 64:((2 + a) * nk + k + 1) * 64]
                    cs, sn = C("cos")[:, a * 64:a * 64 + 64], C("sin")[:, a * 64:a * 64 + 64]
                    ops.append(pool(lambda e, c=c, cs=cs, wk=wk: e.tensor_tensor(c, cs, wk, ALU.mult), waits, ld_c, ld_p))
                    ops.append(pool(lambda e, s=s, sn=sn, wk=wk: e.tensor_tensor(s[:, 0:32], sn[:, 0:32], wk[:, 32:64], ALU.mult)))
                    ops.append(pool(lambda e, s=s, sn=sn, wk=wk: e.tensor_tensor(s[:, 32:64], sn[:, 32:64], wk[:, 0:32], ALU.mult)))
            return ops[-1]

        def rope(src, tab, a, nh, nk, tmp, dst, tab_ready, waits, twice=None):
            per = nh // nk
            sv = src.rearrange("p (k h d) -> p k h d", k=nk, d=64)
            tv = tmp.rearrange("p (k h d) -> p k h d", k=nk, d=64)
            dv = dst.rearrange("p (k h d) -> p k h d", k=nk, d=64)
            muls = []
            for k in range(nk):
                cb = tab[:, (a * nk + k) * 64:(a * nk + k) * 64 + 64]
                sn = tab[:, ((2 + a) * nk + k) * 64:((2 + a) * nk + k) * 64 + 64]
                cbb = cb.rearrange("p (o d) -> p o d", o=1).to_broadcast([P, per, 64])
                s1 = sn[:, 0:32].rearrange("p (o d) -> p o d", o=1).to_broadcast([P, per, 32])
                s2 = sn[:, 32:64].rearrange("p (o d) -> p o d", o=1).to_broadcast([P, per, 32])
                pool(lambda e, k=k, s1=s1: e.tensor_tensor(tv[:, k, :, 0:32], sv[:, k, :, 32:64], s1, ALU.mult), waits, tab_ready)
                m2 = pool(lambda e, k=k, s2=s2: e.tensor_tensor(tv[:, k, :, 32:64], sv[:, k, :, 0:32], s2, ALU.mult))
                m3 = dve(lambda e, k=k, cbb=cbb: e.tensor_tensor(dv[:, k], sv[:, k], cbb, ALU.mult), waits, tab_ready)
                muls.append([m2, m3])
            if twice is not None:
                two = lambda t: t.rearrange("p (h o d) -> p h o d", o=1, d=64).to_broadcast([P, nh, 2, 64])
                return lambda: dve(lambda e: e.tensor_tensor(twice, two(dst), two(tmp), ALU.add), muls)
            return lambda: dve(lambda e: e.tensor_tensor(dst, dst, tmp, ALU.add), muls)

        def head_stats(src, nh, sqbuf, out8, waits, post=None):
            sq = act(lambda e: e.activation(sqbuf, src, ACT.Square, scale=0.125), *waits)
            rd = dve(lambda e: e.tensor_reduce(out8, sqbuf.rearrange("p (h d) -> p h d", d=64), AX, ALU.add), sq)
            return sq, rsqrt(out8, out8, EPS, rd)

        def transpose4(bank, srcs, ready, dst, dst_free):
            for k, s in enumerate(srcs):
                tr = pe(lambda e, k=k, s=s: e.transpose(bank.t[:, k * P:k * P + P], s, ident), ready, bank.free, ld_c)
            ev = act(lambda e: e.activation(dst, bank.t[:, 0:P * len(srcs)].rearrange("p (k t) -> p k t", t=P), ACT.Copy), tr, dst_free)
            bank.free = [ev]
            return ev, tr

        def softmax_heads(jobs, qk_ready, vpad_ready, y_out, rests):
            n = len(jobs)
            mem = {}
            for i in range(n + 2):
                if i < n:
                    J = jobs[i]
                    b = side[i % 2]
                    s1 = pe(lambda e, J=J, b=b: e.matmul(b.t[:, 0:P], J["q"](0, P), J["k"](0, P), start=True, stop=True), b.free, qk_ready)
                    s1 = pe(lambda e, J=J, b=b: e.matmul(b.t[:, P:3 * P], J["q"](P, S), J["k"](0, S), start=True, stop=True))
                    sm, nb, rr = smb[i % 2], small[:, 64 + 8 * (i % 2):64 + 8 * (i % 2) + 8], None
                    cm = C("cmask")
                    fr = smb_free[i % 2]
                    r0 = dve(lambda e, b=b, sm=sm, nb=nb: e.tensor_tensor_reduce(sm[:, 0:P], b.t[:, 0:P], cm[:, 0:P], 1.0, -3.0e38, ALU.add, ALU.max, nb[:, 0:1]), s1, fr)
                    r1 = dve(lambda e, b=b, sm=sm, nb=nb: e.tensor_tensor_reduce(sm[:, P:3 * P], b.t[:, P:3 * P], cm[:, P:3 * P], 1.0, -3.0e38, ALU.add, ALU.max, nb[:, 1:2]))
                    b.free = [r1]
                    n2 = dve(lambda e, J=J, nb=nb: e.tensor_tensor(nb[:, 2:4], nb[:, 0:2], J["nsc"], ALU.mult), r0, r1)
                    pb = pbuf[i % 2]
                    e0 = act(lambda e, J=J, sm=sm, nb=nb, pb=pb: e.activation(pb[:, 0:P], sm[:, 0:P], ACT.Exp, bias=nb[:, 2:3], scale=J["sc"][:, 0:1], accum_out=nb[:, 4:5]), n2, pbuf_free[i % 2])
                    e1 = act(lambda e, J=J, sm=sm, nb=nb, pb=pb: e.activation(pb[:, P:3 * P], sm[:, P:3 * P], ACT.Exp, bias=nb[:, 3:4], scale=J["sc"][:, 1:2], accum_out=nb[:, 5:6]))
                    yield 2
                    rc = dve(lambda e, nb=nb: e.reciprocal(nb[:, 6:8], nb[:, 4:6]), e0, e1)
                    if J["gate"] is not None:
                        rc = dve(lambda e, J=J, nb=nb: e.tensor_tensor(nb[:, 6:8], nb[:, 6:8], J["gate"], ALU.mult), rc)
                    q0 = dve(lambda e, nb=nb, pb=pb: e.tensor_scalar(pb[:, 0:P], pb[:, 0:P], nb[:, 6:7], None, ALU.mult), rc)
                    q1 = dve(lambda e, nb=nb, pb=pb: e.tensor_scalar(pb[:, P:3 * P], pb[:, P:3 * P], nb[:, 7:8], None, ALU.mult))
                    smb_free[i % 2] = [q1]
                    mem[i] = (pb, [q0, q1])
                if 0 <= i - 1 < n:
                    pb, rdy = mem[i - 1]
                    b = side[2]
                    for d, s in ((0, 0), (1, 1), (2, 2)):
                        tr = pe(lambda e, pb=pb, b=b, d=d: e.transpose(b.t[:, d * P:d * P + P], pb[:, d * P:d * P + P], ident), rdy, b.free)
                    pbuf_free[(i - 1) % 2] = [tr]
                    pt = ptb[(i - 1) % 2]
                    ev = act(lambda e, pt=pt, b=b: e.activation(pt[:, :], b.t[:, 0:3 * P], ACT.Copy), tr, ptb_free[(i - 1) % 2])
                    b.free = [ev]
                    mem[i - 1] = (pt, ev)
                if i < 2:
                    yield rests(i)
                if 0 <= i - 2 < n:
                    J = jobs[i - 2]
                    pt, ev = mem.pop(i - 2)
                    b = side[3]
                    o = b.t[:, 0:S]
                    m = pe(lambda e, J=J, pt=pt, o=o: e.matmul(o, J["v"](0), pt[:, 0:S], start=J["first"], stop=False, skip_group_check=True),
                           ev, b.free, vpad_ready)
                    m = pe(lambda e, J=J, pt=pt, o=o: e.matmul(o[:, P:S], J["v"](1), pt[:, S:3 * P], start=False, stop=J["last"] and not J.get("post"), skip_group_check=True))
                    ptb_free[(i - 2) % 2] = [m]
                    if J["last"]:
                        if J.get("post"):
                            m = J["post"](o, b)
                        y_out(J["pair"], b, m)
                    yield rests(i)

        def split_y(blk, src, ready, wait_free):
            hi = act(lambda e: e.activation(yhi[:, blk * S:blk * S + S], src, ACT.Copy), ready, wait_free)
            lo = dve(lambda e: e.tensor_tensor(ylo[:, blk * S:blk * S + S], src, yhi[:, blk * S:blk * S + S].bitcast(F32), ALU.subtract), hi)
            return lo

        R = {}
        o_ = 0
        for nm, n in (("smb", 768), ("pbuf", 768), ("ptb", 768), ("qT", 1024), ("kT", 1024),
                      ("vpad", 2048), ("us", 1024), ("dT", 256), ("tab", 512), ("pool", 1536), ("pw", 512)):
            R[nm] = arena[:, o_:o_ + n]
            o_ += n
        for i, nm in enumerate(("ks", "qs", "tmp", "ro")):
            R[nm] = gates[:, i * 1024:i * 1024 + 1024]
        gates_free = [[]]
        smb = [R["smb"][:, 0:384], R["smb"][:, 384:768]]
        pbuf = [R["pbuf"][:, 0:384], R["pbuf"][:, 384:768]]
        ptb = [R["ptb"][:, 0:384], R["ptb"][:, 384:768]]
        smb_free, pbuf_free, ptb_free = [[], []], [[], []], [[], []]
        scq = small[:, 96:112]
        nscq = small[:, 112:128]
        rk = small[:, 128:144]
        hb16 = small[:, 144:160]
        Y = {"readers": []}

        def ticker(*lists):
            due = [1] * len(lists)
            count = [0]

            def tick():
                count[0] += 1
                ran = False
                for i in range(len(lists)):
                    d = due[i]
                    if not lists[i] or d > count[0] or (ran and d == count[0]):
                        continue
                    ran = True
                    while lists[i]:
                        try:
                            due[i] = max(count[0] + 1, d + (next(lists[i][0]) or 1))
                            break
                        except StopIteration:
                            lists[i].pop(0)
                            d = count[0]

            return tick

        def mixer1(l):
            T = f"L{l}"
            start = [arena_free[0]]
            halfb[0] = pool(lambda e: e.tensor_scalar(hb16, PR(f"bg{l}"), 0.5, None, ALU.mult), ld_p, *gate_ops.get(KD - 1, []))
            tabk, tabq = R["tab"][:, 0:256], R["tab"][:, 256:512]
            tk = rope_tables(tabk, PR(f"kn{l}"), 1, start)
            tq = rope_tables(tabq, PR(f"qn{l}"), 1, ())
            zv = pool(lambda e: e.memset(R["vpad"], 0.0), start)
            bg, bgq = [], []
            tick = ticker(bg, bgq)

            def evac_qk(b, fin, dst, waits):
                ops = []
                for a in range(2):
                    ops.append(act(lambda e, a=a: e.activation(dst[:, a * 512:a * 512 + 512], b[a].t[:, :], ACT.Copy), fin[a], waits))
                    b[a].free = [ops[-1]]
                return ops

            res = {}

            def kq(ev, isq):
                src = R["qs"] if isq else R["ks"]
                sv = [src[:, a * 512:a * 512 + 512] for a in range(2)]
                rv = [R["ro"][:, a * 512:a * 512 + 512] for a in range(2)]
                st8 = [(scq if isq else rk)[:, a * 8:a * 8 + 8] for a in range(2)]
                pre = []
                for a in range(2):
                    sq, rs = head_stats(sv[a], 8, R["tmp"][:, a * 512:a * 512 + 512], st8[a], (ev[a], start, res.get("ro", [])))
                    if isq:
                        r1 = pool(lambda e, a=a: e.tensor_scalar(nscq[:, a * 8:a * 8 + 8], st8[a], -0.125, None, ALU.mult), rs, res.get("nsc", []))
                        r2 = pool(lambda e, a=a: e.tensor_scalar(st8[a], st8[a], 0.125, None, ALU.mult), r1)
                        pre.append([r2, rs, sq])
                        res["sc"] = r2
                    else:
                        pre.append([rs])
                return sv, rv, st8, pre, src

            def to_feat(nm, sv, rv, st8, pre, src, tab, tabr, isq, rest, rest2):
                yield rest
                adds, ros = [], []
                for a in range(2):
                    if not isq:
                        rb = st8[a].rearrange("p (h o) -> p h o", o=1).to_broadcast([P, 8, 64])
                        sv3 = v3d(sv[a], 8, 64)
                        pre[a] = [dve(lambda e, sv3=sv3, rb=rb: e.tensor_tensor(sv3, sv3, rb, ALU.mult), pre[a])]
                    adds.append(rope(sv[a], tab, a, 8, 1, R["tmp"][:, (a * 512):(a * 512) + 512], rv[a], tabr, (pre[a], res.get("ro", []), res.get("ktr", []))))
                    yield
                res["ro"] = ros
                for a in range(2):
                    ros.append(adds[a]())
                    yield
                yield rest2
                for a in range(2):
                    bank = side[a]
                    dT = R[nm + "T"].rearrange("p (k t) -> p k t", t=S)[:, :, a * P:a * P + P]
                    evt, tr = transpose4(bank, [rv[a][:, c * P:c * P + P] for c in range(4)], ros[a], dT, start)
                    res[nm, a] = evt
                    res.setdefault("ktr", []).append(tr)
                    yield 2

            b, fin = tok_group(T + "k", 512, first=True)
            start.append(arena_free[0])
            bg.append(to_feat("k", *kq(evac_qk(b, fin, R["ks"], start), False), tabk, tk, False, 3, 2))
            b, fin = tok_group(T + "q", 512, tick)
            bgq.append(to_feat("q", *kq(evac_qk(b, fin, R["qs"], start), True), tabq, tq, True, 4, 2))
            b, fin = tok_group(T + "u", 512, tick)
            us = R["us"]
            uops = []
            for a in range(2):
                uops.append(act(lambda e, a=a, b=b: e.activation(us[:, a * 512:a * 512 + 512], b[a].t[:, :], ACT.Copy), fin[a], start))
                b[a].free = [uops[-1]]

            def poolers():
                fr = []
                for g in range(4):
                    bank = side[g % 2]
                    pm = R["pool"][:, g * 384:g * 384 + 384]
                    pe(lambda e, g=g, bank=bank, pm=pm: e.matmul(bank.t[:, 0:S], us[:, g * P:g * P + P], pm[:, 0:S], start=True, stop=False, skip_group_check=True),
                       uops, bank.free, pw_ld[0])
                    m = pe(lambda e, g=g, bank=bank, pm=pm: e.matmul(bank.t[:, P:S], us[:, 512 + g * P:512 + g * P + P], pm[:, S:S + P], start=False, stop=True, skip_group_check=True))
                    dT = R["dT"]
                    ev = act(lambda e, bank=bank: e.activation(dT, bank.t[:, 0:S], ACT.Copy), m, fr)
                    bank.free = [ev]
                    yield
                    bank = side[2 + g % 2]
                    m = pe(lambda e, g=g, bank=bank: e.matmul(bank.t[:, 0:S], pw[:, g * P:g * P + P], dT, start=True, stop=True), ev, bank.free, pw_ld[0])
                    fr = [m]
                    sc = PR(f"ps{l}")[:, g:g + 1]
                    dst = yhi[:, g * S:g * S + S]
                    hi = act(lambda e, g=g, bank=bank, sc=sc, dst=dst: e.activation(dst, bank.t[:, 0:S], ACT.Copy, scale=sc), m, Y["readers"])
                    lo = dve(lambda e, g=g, bank=bank, sc=sc, dst=dst: e.scalar_tensor_tensor(ylo[:, g * S:g * S + S], bank.t[:, 0:S], sc, dst.bitcast(F32), ALU.mult, ALU.subtract), hi)
                    bank.free = [lo]
                    res.setdefault("y0", []).append(lo)
                    yield
                pw_free[0] = fr

            bg.append(poolers())
            b, fin = tok_group(T + "v", 512, tick)
            vops = []
            for a in range(2):
                dst = R["vpad"][:, a * 1024:a * 1024 + 1024].rearrange("p (c y) -> p c y", y=256)
                for j in range(2):
                    vops.append(act(lambda e, a=a, j=j, dst=dst, b=b: e.activation(dst[:, :, 192 * j:192 * j + 64],
                                    b[a].t[:, :].rearrange("p (c j d) -> p c j d", j=2, d=64)[:, :, j, :], ACT.Copy), fin[a], zv))
                b[a].free = [vops[-1]]
            def jobs():
                out_ = []
                for h in range(8):
                    c, o = h // 2, 64 * (h % 2)
                    out_.append(dict(
                        q=lambda a, b_, c=c, o=o: R["qT"][o:o + 64, c * S + a:c * S + b_],
                        k=lambda a, b_, c=c, o=o: R["kT"][o:o + 64, c * S + a:c * S + b_],
                        sc=scq.rearrange("p (a h) -> p h a", a=2)[:, h, :], nsc=nscq.rearrange("p (a h) -> p h a", a=2)[:, h, :],
                        v=lambda s, h=h: R["vpad"][:, s * 1024 + h * P:s * 1024 + h * P + P],
                        gate=None, pair=c, first=h % 2 == 0, last=h % 2 == 1))
                return out_

            def y_out(pair, b, m):
                lo = split_y(4 + pair, b.t[:, 0:S], m, Y["readers"])
                b.free = [lo]
                res.setdefault("y1", []).append(lo)

            def attn():
                yield from softmax_heads(jobs(), [res["k", 0], res["k", 1], res["q", 0], res["q", 1], res["sc"]], vops, y_out, lambda i: 1)
            bg.append(attn())
            gates_free[0] = [res["q", 0], res["q", 1]]
            for f in range(KD):
                gmm = gate_block(T, f, hb16, tick)
            while bg or bgq:
                tick()
            H["readers"] = [gmm]
            merge_tail(T, [res["y0"], res["y1"]])

        pw = R["pw"]
        pw_free = [[]]
        pw_ld = [None]

        def load_pool_w(l):
            pw_ld[0] = [Q.dma("ld_pw", lambda e: e.dma_start(pw, par_dram_pw[l]), pw_free[0], arena_free[0]),
                        Q.dma("ld_pm", lambda e: e.dma_start(R["pool"], const_in[:, cat["pool"][0]:cat["pool"][1]]))]

        def mixer2():
            start = [arena_free[0]]
            a0 = lambda lo_, n: arena[:, lo_:lo_ + n]
            kraw, qraw, tmpb, rob = R["ks"], R["qs"], R["tmp"], R["ro"]
            qT, kT, vp, mqk, qkT = a0(2304, 1024), a0(3328, 1024), a0(4352, 1536), a0(5888, 1040), a0(6928, 1024)
            tab, mv, gmo = a0(7952, 1024), a0(8976, 1040), a0(10016, 1024)
            kc2, vc2, X = a0(11040, 512), a0(11552, 512), [kraw[:, 0:480], kraw[:, 480:960]]
            hm = a0(11040, 1024)
            Eb = [a0(12064, 384), a0(12448, 384)]
            Pb = [mqk[:, 0:384], mqk[:, 384:768]]
            Vb, Pc, PcT = tab[:, 0:512], tab[:, 512:768], tab[:, 768:1024]
            w16 = small[:, 176:192]
            gt = small[:, 192:240]
            ifs = small[:, 240:256]
            hc = small[:, 256:376]
            hcT = hm[0:30, 0:512]
            kcT = small[:, 376:406]
            vcs = small[0:15, 408:536]
            acol, ecol = small[:, 536:544], small[:, 544:552]
            ms = small[:, 552:560]
            dcol = small[:, 32:48]
            mx16 = small[:, 16:32]
            rows = [prod[0], prod[1], sil[0], sil[1]]
            row = lambda i: rows[i][0:4, :]
            halfb[0] = pool(lambda e: e.tensor_scalar(hb16, PR("mg"), 0.5, None, ALU.mult), ld_p, *gate_ops[KD - 1])
            tabk, tabq = tab[:, 0:768], tab[:, 768:1024]
            tk = rope_tables(tabk, PR("kn3"), 3, start)
            tq = rope_tables(tabq, PR("qn2"), 1, ())
            z1 = pool(lambda e: e.memset(vp, 0.0), start)
            z2 = pool(lambda e: e.memset(mqk, 0.0), start)
            z3 = pool(lambda e: e.memset(mv, 1.0), start)
            bg, bg2, bg3 = [], [], []
            res = {}

            tick = ticker(bg, bg2, bg3)

            b, fin = tok_group("Mk3", 512, first=True)
            start.append(arena_free[0])
            kev, kvd = [], []
            dup4 = [a0(a * 1024, 1024).rearrange("p (h o d) -> p h o d", o=2, d=64) for a in range(2)]
            for a in range(2):
                kev.append(act(lambda e, a=a, b=b: e.activation(kraw[:, a * 512:a * 512 + 384], b[a].t[:, 0:384], ACT.Copy), fin[a], start))
                kvd.append(act(lambda e, a=a, b=b: e.activation(dup4[a][:, 6:8], b[a].t[:, 384:512].rearrange("p (h o d) -> p h o d", o=1, d=64).to_broadcast([P, 2, 2, 64]), ACT.Copy)))
                b[a].free = [kvd[-1]]
            kst = []
            for a in range(2):
                _, rs = head_stats(kraw[:, a * 512:a * 512 + 384], 6, rob[:, a * 512:a * 512 + 384], rk[:, a * 8:a * 8 + 6], (kev[a], start))
                kst.append(rs)

            def kproc():
                yield 3
                adds, d1s = [], []
                for a in range(2):
                    sv = kraw[:, a * 512:a * 512 + 384]
                    rb = rk[:, a * 8:a * 8 + 6].rearrange("p (h o) -> p h o", o=1).to_broadcast([P, 6, 64])
                    sv3 = v3d(sv, 6, 64)
                    nr = dve(lambda e, sv3=sv3, rb=rb: e.tensor_tensor(sv3, sv3, rb, ALU.mult), kst[a])
                    adds.append(rope(sv, tabk, a, 6, 3, tmpb[:, a * 512:a * 512 + 384], rob[:, a * 512:a * 512 + 384], tk, ([nr],), dup4[a][:, 0:6]))
                    yield
                res["kadd"] = d1s
                for a in range(2):
                    d1s.append(adds[a]())
                    yield
                yield 2
                for a in range(2):
                    d1, d2 = d1s[a], kvd[a]
                    bank = side[a]
                    dup = a0(a * 1024, 1024)
                    for i in range(4):
                        tr = pe(lambda e, i=i, dup=dup, bank=bank: e.transpose(bank.t[:, i * P:i * P + P], dup[:, (2 + i) * P:(3 + i) * P], ident), d1, bank.free)
                    dst = kT.rearrange("p (k t) -> p k t", t=S)[:, :, a * P:a * P + P]
                    ev = act(lambda e, dst=dst, bank=bank: e.activation(dst, bank.t[:, :].rearrange("p (k t) -> p k t", t=P), ACT.Copy), tr, start)
                    bank.free = [ev]
                    res["kT", a] = ev
                    yield
                    for i in range(4):
                        j = i if i < 2 else i + 4
                        tr = pe(lambda e, i=i, j=j, dup=dup, bank=bank: e.transpose(bank.t[:, i * P:i * P + P], dup[:, j * P:j * P + P], ident), d2, bank.free)
                    bv = bank.t[:, :].rearrange("p (k g t) -> p k g t", k=2, g=2)
                    ops = []
                    for k, buf in enumerate((kc2, vc2)):
                        bb = buf.rearrange("p (g t) -> p g t", g=2)
                        s0 = 1 - a
                        ops.append(act(lambda e, bb=bb, k=k, a=a, bv=bv: e.activation(bb[0:64, :, a * P:a * P + P], bv[0:64, k], ACT.Copy), tr, start))
                        ops.append(act(lambda e, bb=bb, k=k, a=a, s0=s0, bv=bv: e.activation(bb[64:P, :, a * P - 1 + s0:a * P + P - 1], bv[64:P, k, :, s0:P], ACT.Copy)))
                    bank.free = ops[-1:]
                    res["c2", a] = ops
                    yield
                yield 2
                for k, (buf, pn) in enumerate(((kc2, "kpe"), (vc2, "vpe"))):
                    xv = X[k].rearrange("p (j g n) -> p j g n", j=16, g=2)
                    for g in range(2):
                        for jh in range(2):
                            in0 = buf[:, g * S:g * S + S].rearrange("p (n j two) -> p j n two", j=8, two=2)[:, :, jh:jh + 15, 0]
                            pb_ = PR(pn)[:, 8 * jh:8 * jh + 8].rearrange("p (j o) -> p j o", o=1).to_broadcast([P, 8, 15])
                            o = pool(lambda e, xv=xv, g=g, jh=jh, in0=in0, pb_=pb_: e.tensor_tensor(xv[:, 8 * jh:8 * jh + 8, g, :], in0, pb_, ALU.add),
                                     res["c2", 0], res["c2", 1], start, ld_p)
                    res.setdefault("X", []).append(o)
                yield

            bg.append(kproc())
            b, fin = tok_group("Mnq", 512, tick)
            qev = []
            for a in range(2):
                qev.append(act(lambda e, a=a, b=b: e.activation(qraw[:, a * 512:a * 512 + 512], b[a].t[:, :], ACT.Copy), fin[a], start))
                b[a].free = [qev[-1]]

            qst = []
            for a in range(2):
                st8 = scq[:, a * 8:a * 8 + 8]
                sq, rs = head_stats(qraw[:, a * 512:a * 512 + 512], 8, rob[:, a * 512:a * 512 + 512], st8, (qev[a], res["kadd"]))
                r1 = pool(lambda e, a=a, st8=st8: e.tensor_scalar(nscq[:, a * 8:a * 8 + 8], st8, -0.125, None, ALU.mult), rs)
                r2 = pool(lambda e, st8=st8: e.tensor_scalar(st8, st8, 0.125, None, ALU.mult), r1)
                res["sc"] = r2
                qst.append([r2, sq])

            def qproc():
                adds, ros = [], []
                for a in range(2):
                    adds.append(rope(qraw[:, a * 512:a * 512 + 512], tabq, a, 8, 1, tmpb[:, a * 512:a * 512 + 512], rob[:, a * 512:a * 512 + 512], tq, (qst[a],)))
                    yield
                for a in range(2):
                    ros.append(adds[a]())
                    yield
                yield 2
                for a in range(2):
                    rv, ro = rob[:, a * 512:a * 512 + 512], ros[a]
                    dT = qT.rearrange("p (k t) -> p k t", t=S)[:, :, a * P:a * P + P]
                    evt, tr = transpose4(side[a], [rv[:, c * P:c * P + P] for c in range(4)], ro, dT, start)
                    res["qT", a] = evt
                    yield

            bg.append(qproc())
            b, fin = tok_group("Mv3", 288, tick)
            vops, gops = [], []
            for a in range(2):
                dst = vp.rearrange("p (k s g y) -> p k s g y", k=2, s=2, g=2)[:, :, a, :, 64:128]
                vops.append(act(lambda e, a=a, b=b, dst=dst: e.activation(dst, b[a].t[:, 0:256].rearrange("p (k g d) -> p k g d", k=2, g=2), ACT.Copy), fin[a], z1))
                i1 = act(lambda e, a=a, b=b: e.activation(ifs[:, a * 8:a * 8 + 8], b[a].t[:, 256:264], ACT.Copy))
                i2 = act(lambda e, a=a, b=b: e.activation(gt[:, a * 24:a * 24 + 24], b[a].t[:, 264:288], ACT.Tanh, scale=0.5))
                b[a].free = [i2]
                gops += [i1, i2]
            gfin = dve(lambda e: e.tensor_scalar(gt, gt, 0.5, 0.5, ALU.mult, ALU.add), gops)

            def lstm_rows():
                bank = side[2]
                for j in range(2):
                    for a in range(2):
                        m = pe(lambda e, j=j, a=a: e.matmul(bank.t[0:4, j * S + a * P:j * S + a * P + P], ifs[:, a * 8 + 4 * j:a * 8 + 4 * j + 4], ident, start=True, stop=True),
                               gops, bank.free)
                r1 = dve(lambda e: e.tensor_scalar(row(0), bank.t[0:4, 0:S], PR("ib")[0:4, :], None, ALU.add), m, ld_p)
                r2 = dve(lambda e: e.tensor_scalar(row(1), bank.t[0:4, S:2 * S], PR("fb")[0:4, :], None, ALU.add))
                bank.free = [r2]
                yield 1
                r3 = act(lambda e: e.activation(row(2), row(1), ACT.Abs), r2)
                r4 = act(lambda e: e.activation(row(2), row(2), ACT.Exp, scale=-1.0), r3)
                r5 = act(lambda e: e.activation(row(2), row(2), ACT.Ln, bias=1.0), r4)
                yield 2
                r6 = dve(lambda e: e.scalar_tensor_tensor(row(1), row(1), 0.0, row(2), ALU.min, ALU.subtract), r5)
                r7 = dve(lambda e: e.memset(row(3), 0.0))
                r8 = dve(lambda e: e.tensor_tensor_scan(row(2), row(1), row(3), 0.0, ALU.add, ALU.add), r6, r7)
                r9 = dve(lambda e: e.tensor_tensor(row(0), row(0), row(2), ALU.subtract), r8, r1)
                yield 1
                r10 = dve(lambda e: e.tensor_tensor_scan(row(1), row(0), row(0), 0.0, ALU.max, ALU.max), r9)
                r11 = dve(lambda e: e.tensor_tensor(row(3), row(2), row(1), ALU.add), r10)
                r12 = act(lambda e: e.activation(row(3), row(3), ACT.Exp, scale=-1.0), r11)
                yield 6
                for a in range(2):
                    pe(lambda e, a=a: e.matmul(bank.t[:, a * 4:a * 4 + 4], rows[0][0:4, a * P:a * P + P], ident[0:4, 0:4], start=True, stop=True), bank.free, r9)
                    m = pe(lambda e, a=a: e.matmul(bank.t[:, 8 + a * 4:12 + a * 4], rows[3][0:4, a * P:a * P + P], ident[0:4, 0:4], start=True, stop=True), r12)
                e1 = dve(lambda e: e.tensor_copy(small[:, 536:552], bank.t[:, 0:16]), m)
                bank.free = [e1]
                res["cols"], res["M"] = e1, r10
                yield

            bg2.append(lstm_rows())
            cbank = side[3]
            w1n = [0]

            def compress_step():
                i = w1n[0]
                w1n[0] += 1
                kv, q = i // 4, i % 4
                t = next_tile(f"M{'kv'[kv]}w1{q}")
                for jj in range(4):
                    j = 4 * q + jj
                    mm = pe(lambda e, t=t, jj=jj, j=j, kv=kv, i=i: e.matmul(
                            cbank.t[0:30, kv * 256:kv * 256 + 256], X[kv][:, j * 30:j * 30 + 30], t.raw[:, jj * 256:jj * 256 + 256],
                            start=(i == 0 and jj == 0), stop=(j == 15), skip_group_check=True),
                            t.ready, res["X"], cbank.free if i == 0 else [])
                release(t, mm)
                res["cmp"] = mm

            def compressed():
                g0 = act(lambda e: e.activation(hcT, cbank.t[0:30, :], ACT.Gelu), res["cmp"])
                cbank.free = [g0]
                yield 3
                bank = side[2]
                for i in range(4):
                    tr = pe(lambda e, i=i: e.transpose(bank.t[:, i * 30:i * 30 + 30], hcT[:, i * P:i * P + P], ident[0:30, 0:30]), g0, bank.free)
                g1 = act(lambda e: e.activation(hc, bank.t[:, 0:120], ACT.Copy), tr)
                bank.free = res["hc"] = [g1]
                yield 2
                for hb_ in range(2):
                    m = pe(lambda e, hb_=hb_: e.matmul(bank.t[:, 0:30], PR("kw2")[:, hb_ * P:hb_ * P + P], hc[:, hb_ * 30:hb_ * 30 + 30], start=hb_ == 0, stop=hb_ == 1),
                           g1, bank.free, ld_p)
                for g in range(2):
                    for hb_ in range(2):
                        m = pe(lambda e, hb_=hb_, g=g: e.matmul(bank.t[0:15, 64 + g * 64:128 + g * 64], hc[:, (2 + hb_) * 30 + g * 15:(2 + hb_) * 30 + g * 15 + 15],
                                                                PR("vw2")[:, hb_ * P:hb_ * P + 64], start=hb_ == 0, stop=hb_ == 1))
                e1 = act(lambda e: e.activation(kcT, bank.t[:, 0:30], ACT.Copy), m)
                e2 = act(lambda e: e.activation(vcs, bank.t[0:15, 64:192], ACT.Copy))
                bank.free = [e2]
                yield 2
                bank = side[2]
                for g in range(2):
                    m = pe(lambda e, g=g, bank=bank: e.matmul(bank.t[:, 256:320], C("rep")[0:15, g * P:g * P + P], vcs[:, g * 64:g * 64 + 64], start=g == 0, stop=g == 1), e2, bank.free)
                e3 = dve(lambda e, bank=bank: e.tensor_tensor(Vb.rearrange("p (b d) -> p b d", d=64), bank.t[:, 256:320].rearrange("p (o d) -> p o d", o=1).to_broadcast([P, 8, 64]),
                                                   C("bd").rearrange("p (b d) -> p b d", d=64), ALU.mult), m, res["qT", 0], res["qT", 1])
                bank.free = [e3]
                yield 1
                cbk = [side[2], side[0]]
                for a in range(2):
                    for h in range(8):
                        c, o, g = h // 2, 64 * (h % 2), h // 4
                        bank = cbk[h % 2]
                        m = pe(lambda e, a=a, h=h, c=c, o=o, g=g, bank=bank: e.matmul(bank.t[:, (a * 8 + h) * 16:(a * 8 + h) * 16 + 15], qT[o:o + 64, c * S + a * P:c * S + a * P + P],
                                kcT[o:o + 64, g * 15:g * 15 + 15], start=True, stop=True), e1, bank.free, [res["qT", 0], res["qT", 1]])
                zc = pool(lambda e: e.memset(Pc, 0.0), res["cmp"], res["qT", 0], res["qT", 1])
                p3 = Pc.rearrange("p (r n) -> p r n", n=16)[:, :, 0:15]
                bc = lambda v: v.rearrange("p (r o) -> p r o", o=1).to_broadcast([P, 16, 15])
                for par_ in range(2):
                    s3 = cbk[par_].t[:, 0:256].rearrange("p (r two n) -> p two r n", n=16, two=2)[:, par_, :, 0:15]
                    pp = Pc.rearrange("p (r two n) -> p two r n", n=16, two=2)[:, par_, :, 0:15]
                    sq_ = scq.rearrange("p (r two) -> p two r", two=2)[:, par_, :]
                    c1 = dve(lambda e, pp=pp, s3=s3, sq_=sq_: e.tensor_tensor(pp, s3, sq_.rearrange("p (r o) -> p r o", o=1).to_broadcast([P, 8, 15]), ALU.mult), m, zc, res["sc"])
                    cbk[par_].free = [c1]
                for a in range(2):
                    pa = p3[:, a * 8:a * 8 + 8, :]
                    mk = C("cmneg")[:, a * 16:a * 16 + 15].rearrange("p (o n) -> p o n", o=1).to_broadcast([P, 8, 15])
                    c2 = dve(lambda e, pa=pa, mk=mk: e.tensor_tensor(pa, pa, mk, ALU.add), c1)
                c3 = dve(lambda e: e.tensor_reduce(mx16, p3, AX, ALU.max), c2)
                c4 = dve(lambda e: e.tensor_tensor(p3, p3, bc(mx16), ALU.subtract), c3)
                c5 = act(lambda e: e.activation(p3, p3, ACT.Exp), c4)
                yield 1
                c6 = dve(lambda e: e.tensor_reduce(mx16, p3, AX, ALU.add), c5)
                c7 = dve(lambda e: e.reciprocal(w16, mx16), c6)
                g0 = gt.rearrange("p (r j) -> p r j", j=3)[:, :, 0]
                c8 = dve(lambda e: e.tensor_tensor(w16, w16, g0, ALU.mult), c7, gfin)
                for a in range(2):
                    pa = p3[:, a * 8:a * 8 + 8, :]
                    mk = C("cm01")[:, a * 16:a * 16 + 15].rearrange("p (o n) -> p o n", o=1).to_broadcast([P, 8, 15])
                    c9 = dve(lambda e, pa=pa, mk=mk: e.tensor_tensor(pa, pa, mk, ALU.mult), c6)
                c10 = dve(lambda e: e.tensor_tensor(p3, p3, bc(w16), ALU.mult), c8, c9)
                yield 2
                bank = side[2]
                for a in range(2):
                    tr = pe(lambda e, a=a, bank=bank: e.transpose(bank.t[:, a * P:a * P + P], Pc[:, a * P:a * P + P], ident), c10, bank.free)
                e4 = act(lambda e, bank=bank: e.activation(PcT, bank.t[:, 0:S], ACT.Copy), tr)
                bank.free = [e4]
                res["Pc"] = [e3, e4]
                yield

            def post_for(pair):
                return lambda o, b: pe(lambda e: e.matmul(o, Vb[:, pair * P:pair * P + P], PcT, start=False, stop=True, skip_group_check=True), res["Pc"])

            def jobs():
                out_ = []
                for c in range(4):
                    for i, (hp, kind) in enumerate(((0, 0), (1, 0), (0, 1), (1, 1))):
                        h, o, g = 2 * c + hp, 64 * hp, c // 2
                        kb = (kind * 2 + g) * S
                        out_.append(dict(
                            q=lambda a, b_, c=c, o=o: qT[o:o + 64, c * S + a:c * S + b_],
                            k=lambda a, b_, kb=kb, o=o: kT[o:o + 64, kb + a:kb + b_],
                            sc=scq.rearrange("p (a h) -> p h a", a=2)[:, h, :], nsc=nscq.rearrange("p (a h) -> p h a", a=2)[:, h, :],
                            v=lambda s, kind=kind, g=g, hp=hp: vp[:, ((kind * 2 + s) * 2 + g) * 192 + 64 * (1 - hp):((kind * 2 + s) * 2 + g) * 192 + 64 * (1 - hp) + P],
                            gate=gt.rearrange("p (a r) -> p r a", a=2)[:, h * 3 + 1 + kind, :],
                            pair=c, first=i == 0, last=i == 3, post=post_for(c)))
                return out_

            def y_out(pair, b, m):
                lo = split_y(4 + pair, b.t[:, 0:S], m, Y["readers"])
                b.free = [lo]
                res.setdefault("y1", []).append(lo)

            def attn():
                yield 4
                yield from softmax_heads(jobs(), [res["kT", 0], res["kT", 1], res["qT", 0], res["qT", 1], res["sc"], gfin], vops, y_out, lambda i: 1)

            cw, cb = PR("cw"), PR("cb")
            convs = []

            tmp_cv = hm[:, 512:512 + S]

            def conv_qk(f):
                bk = work.get()
                mm = feat_block(f"Mqk{f}", bk.t[:, 0:S], bk.free, tick=tick)
                xp = mqk[:, f * 260:f * 260 + 260]
                o = qkT[:, f * S:f * S + S]
                ev = act(lambda e, xp=xp, bk=bk: e.activation(xp[:, 3:259], bk.t[:, 0:S], ACT.Copy), mm, z2)
                bk.free = [ev]
                bg3.append(conv(f, xp, o, ev))

            def conv(f, xp, o, ev):
                th = Eb[f % 2][:, 0:S]
                wide = lambda k: cw[:, 4 * f + k:4 * f + k + 1].to_broadcast([P, S])
                c0 = pool(lambda e: e.tensor_scalar(o, xp[:, 0:S], cw[:, 4 * f:4 * f + 1], cb[:, f:f + 1], ALU.mult, ALU.add), ev, ld_p, start)
                for k in range(1, 4):
                    c1 = pool(lambda e, k=k: e.tensor_tensor(tmp_cv, xp[:, k:k + S], wide(k), ALU.mult), c0, start)
                    c0 = pool(lambda e: e.tensor_tensor(o, o, tmp_cv, ALU.add), c1)
                return conv_end(f, o, th, c0)

            def conv_end(f, o, th, c0):
                yield 4
                t1 = act(lambda e, o=o, th=th: e.activation(th, o, ACT.Tanh, scale=0.5), c0, start, convs[-2:-1])
                convs.append(dve(lambda e, o=o, th=th: e.scalar_tensor_tensor(o, th, 1.0, o, ALU.add, ALU.mult), t1))
                yield

            conv_qk(0)
            for i in range(8):
                compress_step()
                tick()
            bg2.append(compressed())
            bg.append(attn())
            for f in range(1, 4):
                conv_qk(f)

            b, fin = tok_group("Mmv", 512, tick)
            mvo = []
            for a in range(2):
                dst = mv[:, a * 520:a * 520 + 520].rearrange("p (h y) -> p h y", y=130)[:, :, 0:P]
                mvo.append(act(lambda e, a=a, b=b, dst=dst: e.activation(dst, b[a].t[:, :].rearrange("p (h y) -> p h y", y=P), ACT.Copy), fin[a], z3))
                b[a].free = [mvo[-1]]
            mb = [banks[2], banks[3]]
            gate_ring = Ring([banks[0], banks[1]])

            def mlstm():
                mrow = rows[1]
                for h in range(4):
                    c, o = h // 2, 64 * (h % 2)
                    E, PT = Eb[h % 2], Pb[h % 2]
                    bm, bs = mb
                    sel = C("sel")[0:4, h * P:h * P + P]
                    pe(lambda e, sel=sel: e.matmul(bm.t[:, 0:S], sel, mrow[0:4, 0:S], start=True, stop=False, skip_group_check=True), res["M"], bm.free)
                    pe(lambda e, sel=sel: e.matmul(bm.t[:, S:S + P], sel, mrow[0:4, P:S], start=False, stop=False, skip_group_check=True))
                    pe(lambda e: e.matmul(bm.t[:, 0:P], ident, C("bigT"), start=False, stop=False, skip_group_check=True))
                    m1 = pe(lambda e: e.matmul(bm.t[:, S:S + P], ident, C("bigT"), start=False, stop=True, skip_group_check=True))
                    e0 = act(lambda e, h=h, E=E: e.activation(E[:, 0:S], bm.t[:, 0:S], ACT.Exp, scale=-1.0, bias=acol[:, h:h + 1]), m1, res["cols"], convs, res.get(("mv", h % 2), []))
                    e1 = act(lambda e, h=h, E=E: e.activation(E[:, S:S + P], bm.t[:, S:S + P], ACT.Exp, scale=-1.0, bias=acol[:, 4 + h:5 + h]))
                    bm.free = [e1]
                    kk, qq = qkT[o:o + 64, (2 + c) * S:(3 + c) * S], qkT[o:o + 64, c * S:(c + 1) * S]
                    pe(lambda e, kk=kk, qq=qq: e.matmul(bs.t[:, 0:S], kk[:, 0:P], qq, start=True, stop=True, skip_group_check=True), convs, bs.free)
                    m2 = pe(lambda e, kk=kk, qq=qq: e.matmul(bs.t[:, S:S + P], kk[:, P:S], qq[:, P:S], start=True, stop=True, skip_group_check=True))
                    yield
                    p1 = dve(lambda e, E=E, PT=PT: e.scalar_tensor_tensor(PT, bs.t[:, 0:S + P], 1.0 / 32, E, ALU.mult, ALU.mult), m2, e0, e1, res.get(("mv", h % 2), []))
                    bs.free = [p1]
                    res["mv", h % 2] = [p1]
                    yield 2
                    ve = lambda a, h=h: mv[:, a * 520 + h * 130:a * 520 + h * 130 + 130]
                    pe(lambda e, PT=PT, ve=ve: e.matmul(bm.t[:, 0:130], PT[:, 0:P], ve(0), start=True, stop=True), p1, mvo, bm.free)
                    pe(lambda e, PT=PT, ve=ve: e.matmul(bm.t[:, 130:260], PT[:, P:S], ve(0), start=True, stop=False))
                    m3 = pe(lambda e, PT=PT, ve=ve: e.matmul(bm.t[:, 130:260], PT[:, S:S + P], ve(1), start=False, stop=True))
                    res["mv", h % 2] = [p1, m3]
                    den = bm.t[:, 0:260].rearrange("p (a y) -> p a y", a=2)[:, :, P]
                    ec = ecol.rearrange("p (a h) -> p h a", a=2)[:, h, :]
                    d2 = dcol[:, 4 * h:4 * h + 2]
                    d0 = dve(lambda e, den=den, ec=ec, d2=d2: e.scalar_tensor_tensor(d2, den, -1.0, ec, ALU.mult, ALU.max), m3, res["cols"])
                    d1 = dve(lambda e, den=den, d2=d2: e.tensor_tensor(d2, den, d2, ALU.max), d0)
                    dr = dve(lambda e, d2=d2: e.reciprocal(d2, d2), d1)
                    for a in range(2):
                        ha = hm[:, a * 512 + h * P:a * 512 + h * P + P]
                        n1 = dve(lambda e, a=a, ha=ha, d2=d2: e.tensor_scalar(ha, bm.t[:, a * 130:a * 130 + P], d2[:, a:a + 1], None, ALU.mult), dr, res["X"], res["hc"])
                        s1 = act(lambda e, a=a, h=h, ha=ha, E=E: e.activation(E[:, a * P:a * P + P], ha, ACT.Square, accum_out=ms[:, a * 4 + h:a * 4 + h + 1]), n1, p1)
                    bm.free = [n1]
                    res["mv", h % 2] = [p1, m3, s1]
                    yield 2
                k1 = pool(lambda e: e.tensor_scalar(ms, ms, 4.0 / 128, None, ALU.mult), s1)
                rs = rsqrt(ms, ms, 4 * EPS, k1)
                n2s = []
                for a in range(2):
                    for h in range(4):
                        ha = hm[:, a * 512 + h * P:a * 512 + h * P + P]
                        n2 = dve(lambda e, a=a, h=h, ha=ha: e.scalar_tensor_tensor(ha, ha, ms[:, a * 4 + h:a * 4 + h + 1], gmo[:, a * 512 + h * P:a * 512 + h * P + P], ALU.mult, ALU.mult), rs, gm)
                    n2s.append(n2)
                yield 4
                for a in range(2):
                    n2, bank = n2s[a], mb[a]
                    for h in range(4):
                        tr = pe(lambda e, a=a, h=h, bank=bank: e.transpose(bank.t[:, h * P:h * P + P], hm[:, a * 512 + h * P:a * 512 + h * P + P], ident), n2, bank.free)
                    dst = lambda buf, a=a: buf[:, 0:4 * S].rearrange("p (k t) -> p k t", t=S)[:, :, a * P:a * P + P]
                    src = bank.t[:, :].rearrange("p (k t) -> p k t", t=P)
                    hi = act(lambda e, dst=dst, src=src: e.activation(dst(yhi), src, ACT.Copy), tr, Y["readers"])
                    lo = dve(lambda e, dst=dst, src=src: e.tensor_tensor(dst(ylo), src, dst(yhi).bitcast(F32), ALU.subtract), hi)
                    bank.free = [lo]
                    res.setdefault("y0", []).append(lo)
                    yield

            bg2.append(mlstm())
            work.items, keep = gate_ring.items, work.items
            b, fin = tok_group("Mmo", 512, tick)
            gm = []
            for a in range(2):
                g = gmo[:, a * 512:a * 512 + 512]
                t1 = act(lambda e, a=a, b=b, g=g: e.activation(g, b[a].t[:, :], ACT.Tanh, scale=0.5), fin[a], start)
                b[a].free = [t1]
                gm.append(dve(lambda e, g=g: e.scalar_tensor_tensor(g, g, 1.0, PR("on"), ALU.add, ALU.mult), t1))

            gates_free[0] = [res["cmp"], res["qT", 0], res["qT", 1]]
            for f in range(KD):
                gmm = gate_block("M", f, hb16, tick)
            while bg or bg2 or bg3:
                tick()
            work.items = keep
            H["readers"] = [gmm]
            merge_tail("M", [[res["y0"], [], [], []], res["y1"]])

        fw, fb = PR("fw"), PR("fbias")
        pads = Ring([Bank(arena[:, 4096:4096 + 258]), Bank(arena[:, 4360:4360 + 258])])
        cvb = Ring([Bank(arena[:, 4624:4624 + S]), Bank(arena[:, 4880:4880 + S])])

        def conv_hidden(i, b, up):
            s, p, ap, cv = sil_ring.get(), prod_ring.get(), pads.get(), cvb.get()
            a1 = act(lambda e: e.activation(ap.t[:, 2:258], b.t[:, 0:S], ACT.Copy), up, ap.free)
            c1 = dve(lambda e: e.tensor_scalar(cv.t, ap.t[:, 2:258], fw[:, 3 * i + 2:3 * i + 3], fb[:, i:i + 1], ALU.mult, ALU.add), a1, cv.free)
            c2 = dve(lambda e: e.scalar_tensor_tensor(cv.t, ap.t[:, 1:257], fw[:, 3 * i + 1:3 * i + 2], cv.t, ALU.mult, ALU.add), c1)
            c3 = dve(lambda e: e.scalar_tensor_tensor(cv.t, ap.t[:, 0:S], fw[:, 3 * i:3 * i + 1], cv.t, ALU.mult, ALU.add), c2)
            ap.free = [c3]
            g1 = act(lambda e: e.activation(s.t[:, :], cv.t, ACT.Gelu), c3, s.free)
            cv.free = [g1]
            m1 = dve(lambda e: e.tensor_tensor(p.t[:, :], s.t[:, :], b.t[:, S:2 * S], ALU.mult), g1, p.free)
            b.free, s.free = [m1], [m1]
            hb, lo = split_hidden(p.t[:, :], m1)
            p.free = [lo]
            return hb, lo

        par_dram_pw = [gains[8 + l][:, 0:512] for l in range(2)]
        xn0 = stage_n(0, [stage_x(0, h, 1.0, ready=ld_x[0]) for h in range(2)])
        pump(0)
        finish_splits(0)
        stage_t(0, xn0)
        pump(1)
        finish_splits(1)
        xn1 = stage_n(1, [stage_x(1, h, 1.0, ready=ld_x[1]) for h in range(2)])
        second_half(xn1)
        for l in range(2):
            ffn(f"L{l}f1", swiglu_hidden, 0.5)
            load_pool_w(l)
            mixer1(l)
            ffn(f"L{l}f2", swiglu_hidden, 0.5)
        mixer2()
        zp = [pool(lambda e, q=q: e.memset(q.t, 0.0), arena_free[0]) for q in pads.items]
        for q in pads.items:
            q.free = zp
        ffn("Mf", conv_hidden, 1.0, True, False)
        Q.put("sp", lambda e: e.nop(), stores)
        Q.number()
        names = sorted({op.sem for q in Q.q.values() for op in q if op.signals})
        sems = {s: ctx.enter_context(nc.semaphore(f"s_{s}")) for s in names}
        block = ctx.enter_context(nc.Block())

        @block.sync
        def _(e):
            Q.run("sp", e, sems)

        @block.scalar
        def _(e):
            Q.run("act", e, sems)

        @block.vector
        def _(e):
            Q.run("dve", e, sems)

        @block.tensor
        def _(e):
            Q.run("pe", e, sems)

        @block.gpsimd
        def _(e):
            Q.run("pool", e, sems)



def kmajor(w, k0=0, nk=KD):
    return w[k0 * P:(k0 + nk) * P].reshape(nk, P, -1).transpose(1, 0, 2).reshape(P, -1)


def pack_weights(I, plan):
    g = lambda n: np.asarray(I[n])
    src = {}

    def ffn(tag, wu, wd):
        w4 = np.concatenate([wu[:, :P], wu[:, DFF:DFF + P], wu[:, P:2 * P], wu[:, DFF + P:DFF + 2 * P]], 1)
        group(f"{tag}p", w4)
        for i in range(NF):
            src[f"{tag}a{i}"] = lambda i=i: kmajor(wu[:, i * P:(i + 1) * P])
            src[f"{tag}b{i}"] = lambda i=i: kmajor(wu[:, DFF + i * P:DFF + (i + 1) * P])
            src[f"{tag}d{i}"] = lambda i=i: wd[i * P:(i + 1) * P]

    def tail(tag, w0, w1, wo):
        for i in range(KD):
            src[f"{tag}br{i}"] = lambda i=i: np.concatenate([kmajor(w0[:, i * P:(i + 1) * P], 0, 4), kmajor(w1[:, i * P:(i + 1) * P], 0, 4)], 1)
            src[f"{tag}wo{i}"] = lambda i=i: wo[i * P:(i + 1) * P]

    def group(tag, w):
        for k, m in a_group(w.shape[1]):
            src[f"{tag}{k}"] = lambda k=k, m=m: kmajor(w, k, m)

    for l in range(2):
        ffn(f"L{l}f1", g("ffn1_w_gate_up")[l], g("ffn1_w_down")[l])
        ffn(f"L{l}f2", g("ffn2_w_gate_up")[l], g("ffn2_w_down")[l])
        wi = g("w_in")[l]
        for j, nm in enumerate("uqkv"):
            group(f"L{l}{nm}", wi[:, j * 512:(j + 1) * 512])
        for f in range(KD):
            for j in range(2):
                src[f"L{l}g{j}{f}"] = lambda wi=wi, f=f, j=j: kmajor(wi[:, 2048 + j * D + f * P:2048 + j * D + (f + 1) * P])
        tail(f"L{l}", g("w_branch_pool")[l], g("w_branch_attn")[l], g("w_out")[l])
    w2 = g("w_in_2")[0]
    col = lambda a, n: w2[:, a:a + n]
    group("Mk3", np.concatenate([col(2056, 128), col(2312, 128), col(2568, 128), col(2184, 128)], 1))
    group("Mv3", np.concatenate([col(2440, 128), col(2696, 128), col(1536, 8), col(2824, 24)], 1))
    group("Mnq", col(1544, 512))
    group("Mmv", col(512, 512))
    group("Mmo", col(1024, 512))
    for f in range(4):
        src[f"Mqk{f}"] = lambda f=f: kmajor(w2[:, f * P:(f + 1) * P])
    for f in range(KD):
        for j in range(2):
            src[f"Mg{j}{f}"] = lambda f=f, j=j: kmajor(w2[:, 2848 + j * D + f * P:2848 + j * D + (f + 1) * P])
    for nm in "kv":
        w1 = g(f"cmp_{nm}_w1_2")[0]
        for i in range(4):
            src[f"M{nm}w1{i}"] = lambda w1=w1, i=i: kmajor(w1, 4 * i, 4)
    tail("M", g("w_up_m_2")[0], g("w_up_n_2")[0], g("w_out_2")[0])
    ffn("Mf", g("ffn_w_up_2")[0], g("ffn_w_down_2")[0])
    total = plan[-1][3] + plan[-1][1]
    out = np.empty(total * P, np.float32)
    for name, n, _, off in plan:
        out[off * P:(off + n) * P] = src[name]().reshape(-1)
    return out


def pack_params(I, pat, n):
    g = lambda k: np.asarray(I[k])
    out = np.zeros((P, n), np.float32)

    def put(name, a):
        out[:a.shape[0], pat[name][0]:pat[name][1]] = a

    cols = lambda v: v.reshape(-1, P).T
    rows = lambda v: np.broadcast_to(v.reshape(1, -1), (P, v.size))
    for l in range(2):
        put(f"bg{l}", cols(g("b_gate")[l]))
        put(f"ps{l}", cols(g("pool_scale")[l]))
        put(f"qn{l}", rows(g("q_norm")[l]))
        put(f"kn{l}", rows(g("k_norm")[l]))
    put("mg", cols(g("merge_gate_b_2")[0]))
    put("cw", g("m_conv_w_2")[0].reshape(4, 4, P).transpose(2, 1, 0).reshape(P, 16))
    put("cb", cols(g("m_conv_b_2")[0]))
    put("ib", g("m_igate_b_2")[0].reshape(4, 1))
    put("fb", g("m_fgate_b_2")[0].reshape(4, 1))
    put("on", rows(g("m_out_norm_w_2")[0]))
    put("qn2", rows(g("q_norm_w_2")[0]))
    put("kn3", np.concatenate([rows(g(k)[0]) for k in ("kcmp_norm_w_2", "kslc_norm_w_2", "kwin_norm_w_2")], 1))
    put("kpe", g("cmp_k_pe_2")[0].reshape(16, P).T)
    put("vpe", g("cmp_v_pe_2")[0].reshape(16, P).T)
    put("fw", g("ffn_conv_w_2")[0].reshape(3, NF, P).transpose(2, 1, 0).reshape(P, -1))
    put("fbias", cols(g("ffn_conv_b_2")[0]))
    kw2, vw2 = g("cmp_k_w2_2")[0], g("cmp_v_w2_2")[0]
    put("kw2", np.concatenate([kw2[0:P], kw2[0:P], kw2[P:], kw2[P:]], 1))
    put("vw2", np.concatenate([vw2[0:P], vw2[0:P], vw2[P:], vw2[P:]], 1))
    return out


def pack_gains(I):
    g = lambda k: np.asarray(I[k])
    rows = [g("ffn1_norm")[0], g("mix_norm")[0], g("ffn2_norm")[0], g("ffn1_norm")[1], g("mix_norm")[1], g("ffn2_norm")[1],
            g("norm1_w_2")[0], g("norm2_w_2")[0]]
    out = np.zeros((10, P, D), np.float32)
    for i, r in enumerate(rows):
        out[i] = r.reshape(1, -1)
    for l in range(2):
        out[8 + l, :, 0:512] = g("pool_w")[l].transpose(1, 0, 2).reshape(P, 512)
    return out


def kernel(**inputs):
    import concourse.bacc as _bacc
    from concourse.bass_utils import run_bass_kernel_spmd as _run

    nc = _bacc.Bacc("TRN2", target_bir_lowering=False, num_devices=1)
    const, cat = constants()
    pat, npar = params_layout()
    plan, _ = tile_plan()
    arrays = {
        "x_dram": np.ascontiguousarray(np.asarray(inputs["x"]).reshape(S, D)),
        "w_dram": pack_weights(inputs, plan),
        "g_dram": pack_gains(inputs),
        "c_dram": const,
        "p_dram": pack_params(inputs, pat, npar),
    }
    aps = {n: nc.dram_tensor(n, a.shape, mybir.dt.float32, kind="ExternalInput").ap() for n, a in arrays.items()}
    out = nc.dram_tensor("out_dram", (S, D), mybir.dt.float32, kind="ExternalOutput").ap()
    build_program(nc, aps["x_dram"], aps["w_dram"], aps["g_dram"], aps["c_dram"], aps["p_dram"], out, cat, pat, plan)
    r = _run(nc, [arrays], core_ids=[0])
    return r.results[0]["out_dram"].reshape(1, S, D)
```
